# Optimizing a Trainium2 kernel written in Bass

```python
import jax
import jax.numpy as jnp
from jax import lax
import numpy as np

D_MODEL = 2048
BATCH = 1
SEQ = 256
DEPTH = 1

NSA_HEADS = 16
NSA_GROUPS = 4
NSA_HEADS_PER_GROUP = NSA_HEADS // NSA_GROUPS
NSA_HEAD_DIM = 64
NSA_ROPE_DIM = NSA_HEAD_DIM // 4
CMP_BLOCK = 32
CMP_STRIDE = 16
CMP_HIDDEN = 256
SEL_BLOCK = 64
SEL_TOPK = 16
WINDOW = 512
N_NSA_BRANCHES = 3
MLA_HEADS = 16
MLA_Q_RANK = 512
MLA_KV_RANK = 256
MLA_NOPE_DIM = 64
MLA_ROPE_DIM = 32
MLA_V_DIM = 64
PEER_HEADS = 8
PEER_N_KEYS = 128
PEER_N_EXPERTS = PEER_N_KEYS * PEER_N_KEYS
PEER_QUERY_DIM = 256
PEER_TOPK = 16
PEER_TOKEN_BLOCK = 128
N_BRANCHES = 2
ROPE_THETA = 500000.0
NORM_EPS = 1e-6
Q_BLOCK = 128
SEL_Q_BLOCK = 32
NEG_INF = -1e30
FORCE_BONUS = 1e4

IN_SIZES = (NSA_HEADS * NSA_HEAD_DIM,
            N_NSA_BRANCHES * 2 * NSA_GROUPS * NSA_HEAD_DIM,
            N_NSA_BRANCHES * NSA_HEADS,
            MLA_Q_RANK,
            MLA_KV_RANK,
            MLA_ROPE_DIM,
            N_BRANCHES * D_MODEL)
IN_COLS = sum(IN_SIZES)

kernel_name = 'hybrid_nsa_mla_peer_block'

def rms_norm(x, g):
    xf = x.astype(jnp.float32)
    y = xf * lax.rsqrt(jnp.mean(xf * xf, axis=-1, keepdims=True) + NORM_EPS)
    return (y * g.astype(jnp.float32)).astype(x.dtype)

def masked_softmax(s, mask):
    s = jnp.where(mask, s.astype(jnp.float32), NEG_INF)
    return jax.nn.softmax(s, axis=-1) * mask

def apply_rope(x, positions, rot_dim):
    half = rot_dim // 2
    inv_freq = ROPE_THETA ** (-jnp.arange(half, dtype=jnp.float32) * (2.0 / rot_dim))
    ang = positions.astype(jnp.float32)[:, :, None] * inv_freq
    cos = jnp.cos(ang)[:, :, None, :]
    sin = jnp.sin(ang)[:, :, None, :]
    xr = x[..., :rot_dim].astype(jnp.float32)
    x1, x2 = xr[..., :half], xr[..., half:]
    rot = jnp.concatenate([x1 * cos - x2 * sin, x2 * cos + x1 * sin], axis=-1)
    return jnp.concatenate([rot.astype(x.dtype), x[..., rot_dim:]], axis=-1)

def map_query_blocks(fn, seq_len, block):
    starts = jnp.arange(seq_len // block, dtype=jnp.int32) * block
    out = lax.map(fn, starts)

    def merge(a):
        a = jnp.moveaxis(a, 0, 1)
        return a.reshape((a.shape[0], seq_len) + a.shape[3:])
    return jax.tree_util.tree_map(merge, out)

def compress_blocks(kraw, pe, w1, b1, w2):
    B, T, G, d = kraw.shape
    n_cmp = (T - CMP_BLOCK) // CMP_STRIDE + 1
    idx = jnp.arange(n_cmp)[:, None] * CMP_STRIDE + jnp.arange(CMP_BLOCK)[None, :]
    blk = kraw[:, idx] + pe[:, None, :]
    blk = jnp.transpose(blk, (0, 1, 3, 2, 4)).reshape(B, n_cmp, G, CMP_BLOCK * d)
    return jax.nn.gelu(blk @ w1 + b1) @ w2

def nsa_attention(q_in, kv_in, gate_in, positions, cmp_pe, cmp_w1, cmp_b1, cmp_w2):
    B, T, _ = q_in.shape
    dt = q_in.dtype
    G, R, d = NSA_GROUPS, NSA_HEADS_PER_GROUP, NSA_HEAD_DIM
    scale = d ** -0.5
    q = apply_rope(q_in.reshape(B, T, NSA_HEADS, d), positions, NSA_ROPE_DIM).reshape(B, T, G, R, d)
    kv = kv_in.reshape(B, T, N_NSA_BRANCHES, 2, G, d)
    k_cmp = compress_blocks(apply_rope(kv[:, :, 0, 0], positions, NSA_ROPE_DIM),
                            cmp_pe[0], cmp_w1[0], cmp_b1[0], cmp_w2[0])
    v_cmp = compress_blocks(kv[:, :, 0, 1], cmp_pe[1], cmp_w1[1], cmp_b1[1], cmp_w2[1])
    k_sel = apply_rope(kv[:, :, 1, 0], positions, NSA_ROPE_DIM)
    v_sel = kv[:, :, 1, 1]
    k_win = apply_rope(kv[:, :, 2, 0], positions, NSA_ROPE_DIM)
    v_win = kv[:, :, 2, 1]

    n_cmp = k_cmp.shape[1]
    n_sel = T // SEL_BLOCK
    n_top = min(SEL_TOPK, n_sel)
    cmp_start = jnp.arange(n_cmp, dtype=jnp.int32) * CMP_STRIDE
    cmp_end = cmp_start + CMP_BLOCK - 1
    sel_start = jnp.arange(n_sel, dtype=jnp.int32) * SEL_BLOCK
    overlap = ((cmp_start[:, None] < sel_start[None, :] + SEL_BLOCK)
               & (cmp_end[:, None] >= sel_start[None, :])).astype(jnp.float32)
    blk_id = jnp.arange(n_sel, dtype=jnp.int32)
    k_blk = jnp.transpose(k_sel.reshape(B, n_sel, SEL_BLOCK, G, d), (0, 3, 1, 2, 4))
    v_blk = jnp.transpose(v_sel.reshape(B, n_sel, SEL_BLOCK, G, d), (0, 3, 1, 2, 4))
    b_ix = jnp.arange(B)[:, None, None, None]
    g_ix = jnp.arange(G)[None, None, :, None]
    in_blk = jnp.arange(SEL_BLOCK, dtype=jnp.int32)

    def cmp_sel_block(s):
        qb = lax.dynamic_slice_in_dim(q, s, SEL_Q_BLOCK, axis=1)
        t = s + jnp.arange(SEL_Q_BLOCK, dtype=jnp.int32)
        sc = jnp.einsum('bqgrd,bngd->bgrqn', qb, k_cmp) * scale
        p_cmp = masked_softmax(sc, cmp_end[None, :] <= t[:, None])
        o_cmp = jnp.einsum('bgrqn,bngd->bqgrd', p_cmp.astype(dt), v_cmp)
        imp = jnp.einsum('bgrqn,ns->bqgs', p_cmp, overlap)
        t_blk = t // SEL_BLOCK
        forced = ((blk_id[None, :] == 0) | (blk_id[None, :] == t_blk[:, None])
                  | (blk_id[None, :] == t_blk[:, None] - 1))
        valid = sel_start[None, :] <= t[:, None]
        imp = jnp.where(valid[None, :, None, :], imp + FORCE_BONUS * forced[None, :, None, :], NEG_INF)
        _, sel = lax.top_k(imp, n_top)
        kg = k_blk[b_ix, g_ix, sel]
        vg = v_blk[b_ix, g_ix, sel]
        tok = sel[..., None] * SEL_BLOCK + in_blk
        smask = (tok <= t[None, :, None, None, None]).reshape(B, SEL_Q_BLOCK, G, 1, n_top * SEL_BLOCK)
        ss = jnp.einsum('bqgrd,bqgkld->bqgrkl', qb, kg) * scale
        p_sel = masked_softmax(ss.reshape(B, SEL_Q_BLOCK, G, R, n_top * SEL_BLOCK), smask)
        o_sel = jnp.einsum('bqgrm,bqgmd->bqgrd', p_sel.astype(dt),
                           vg.reshape(B, SEL_Q_BLOCK, G, n_top * SEL_BLOCK, d))
        return o_cmp, o_sel

    k_pad = jnp.pad(k_win, ((0, 0), (WINDOW, 0), (0, 0), (0, 0)))
    v_pad = jnp.pad(v_win, ((0, 0), (WINDOW, 0), (0, 0), (0, 0)))

    def win_block(s):
        qb = lax.dynamic_slice_in_dim(q, s, Q_BLOCK, axis=1)
        kb = lax.dynamic_slice_in_dim(k_pad, s, WINDOW + Q_BLOCK, axis=1)
        vb = lax.dynamic_slice_in_dim(v_pad, s, WINDOW + Q_BLOCK, axis=1)
        t = s + jnp.arange(Q_BLOCK, dtype=jnp.int32)
        j = s - WINDOW + jnp.arange(WINDOW + Q_BLOCK, dtype=jnp.int32)
        band = (j[None, :] >= 0) & (j[None, :] <= t[:, None]) & (t[:, None] - j[None, :] < WINDOW)
        sc = jnp.einsum('bqgrd,bkgd->bqgrk', qb, kb) * scale
        p = masked_softmax(sc, band[None, :, None, None, :])
        return jnp.einsum('bqgrk,bkgd->bqgrd', p.astype(dt), vb)

    o_cmp, o_sel = map_query_blocks(cmp_sel_block, T, SEL_Q_BLOCK)
    o_win = map_query_blocks(win_block, T, Q_BLOCK)
    g = jax.nn.sigmoid(gate_in.astype(jnp.float32)).astype(dt).reshape(B, T, G, R, N_NSA_BRANCHES)
    o = g[..., 0:1] * o_cmp + g[..., 1:2] * o_sel + g[..., 2:3] * o_win
    return o.reshape(B, T, NSA_HEADS * d)

def mla_attention(c_q, c_kv, k_r, positions, q_norm_g, w_q_up, kv_norm_g, w_kv_up):
    B, T, _ = c_q.shape
    dt = c_q.dtype
    H = MLA_HEADS
    scale = (MLA_NOPE_DIM + MLA_ROPE_DIM) ** -0.5
    q = (rms_norm(c_q, q_norm_g) @ w_q_up).reshape(B, T, H, MLA_NOPE_DIM + MLA_ROPE_DIM)
    q_nope = q[..., :MLA_NOPE_DIM]
    q_rope = apply_rope(q[..., MLA_NOPE_DIM:], positions, MLA_ROPE_DIM)
    kv = (rms_norm(c_kv, kv_norm_g) @ w_kv_up).reshape(B, T, H, MLA_NOPE_DIM + MLA_V_DIM)
    k_nope = kv[..., :MLA_NOPE_DIM]
    v = kv[..., MLA_NOPE_DIM:]
    k_rope = apply_rope(k_r[:, :, None, :], positions, MLA_ROPE_DIM)[:, :, 0]
    key_pos = jnp.arange(T, dtype=jnp.int32)

    def mla_block(s):
        qn = lax.dynamic_slice_in_dim(q_nope, s, Q_BLOCK, axis=1)
        qr = lax.dynamic_slice_in_dim(q_rope, s, Q_BLOCK, axis=1)
        t = s + jnp.arange(Q_BLOCK, dtype=jnp.int32)
        sc = (jnp.einsum('bqhd,bkhd->bhqk', qn, k_nope)
              + jnp.einsum('bqhd,bkd->bhqk', qr, k_rope)) * scale
        p = masked_softmax(sc, (key_pos[None, :] <= t[:, None])[None, None])
        return jnp.einsum('bhqk,bkhd->bqhd', p.astype(dt), v)

    o = map_query_blocks(mla_block, T, Q_BLOCK)
    return o.reshape(B, T, H * MLA_V_DIM)

def token_mixer(h, positions, w_in, cmp_pe, cmp_w1, cmp_b1, cmp_w2, mla_q_norm_g, mla_w_q_up,
                mla_kv_norm_g, mla_w_kv_up, w_branch_nsa, w_branch_mla, w_out):
    B, T, _ = h.shape
    dt = h.dtype
    proj = h @ w_in
    parts = []
    off = 0
    for n in IN_SIZES:
        parts.append(proj[..., off:off + n])
        off += n
    q_nsa, kv_nsa, g_nsa, c_q, c_kv, k_r, g_merge = parts
    o_nsa = nsa_attention(q_nsa, kv_nsa, g_nsa, positions, cmp_pe, cmp_w1, cmp_b1, cmp_w2)
    o_mla = mla_attention(c_q, c_kv, k_r, positions, mla_q_norm_g, mla_w_q_up, mla_kv_norm_g, mla_w_kv_up)
    gates = jax.nn.sigmoid(g_merge.astype(jnp.float32)).astype(dt).reshape(B, T, N_BRANCHES, D_MODEL)
    merged = gates[:, :, 0] * (o_nsa @ w_branch_nsa) + gates[:, :, 1] * (o_mla @ w_branch_mla)
    return merged @ w_out

def peer_ffn(h, w_q, sub_keys, u, v):
    B, T, D = h.shape
    dt = h.dtype
    half = PEER_QUERY_DIM // 2
    qry = (h @ w_q).reshape(B, T, PEER_HEADS, 2, half)
    s = jnp.einsum('bthpd,hpnd->bthpn', qry, sub_keys).astype(jnp.float32)
    s1, i1 = lax.top_k(s[:, :, :, 0], PEER_TOPK)
    s2, i2 = lax.top_k(s[:, :, :, 1], PEER_TOPK)
    n_cand = PEER_TOPK * PEER_TOPK
    cand_s = (s1[..., :, None] + s2[..., None, :]).reshape(B, T, PEER_HEADS, n_cand)
    cand_i = (i1[..., :, None] * PEER_N_KEYS + i2[..., None, :]).reshape(B, T, PEER_HEADS, n_cand)
    top_s, pos = lax.top_k(cand_s, PEER_TOPK)
    expert = jnp.take_along_axis(cand_i, pos, axis=-1)
    gate = jax.nn.softmax(top_s, axis=-1).astype(dt)
    n_tok = B * T
    n_pick = PEER_HEADS * PEER_TOPK
    hf = h.reshape(n_tok, D)
    ef = expert.reshape(n_tok, n_pick)
    gf = gate.reshape(n_tok, n_pick)

    def expert_block(s0):
        hs = lax.dynamic_slice_in_dim(hf, s0, PEER_TOKEN_BLOCK, 0)
        es = lax.dynamic_slice_in_dim(ef, s0, PEER_TOKEN_BLOCK, 0)
        gs = lax.dynamic_slice_in_dim(gf, s0, PEER_TOKEN_BLOCK, 0)
        act = jax.nn.gelu(jnp.einsum('cd,ced->ce', hs, u[es]))
        return jnp.einsum('ce,ced->cd', gs * act, v[es])

    starts = jnp.arange(n_tok // PEER_TOKEN_BLOCK, dtype=jnp.int32) * PEER_TOKEN_BLOCK
    y = lax.map(expert_block, starts)
    return y.reshape(B, T, D)

def setup_inputs(seed: int = 0) -> dict:
    key = jax.random.key(seed)
    ks = jax.random.split(key, 26)
    L, D = DEPTH, D_MODEL

    def nrm(k, shape, scale):
        return jax.random.normal(k, shape, jnp.float32) * scale

    def gain(k, shape):
        return 1.0 + 0.01 * jax.random.normal(k, shape, jnp.float32)

    offset = jax.random.randint(ks[2], (BATCH, 1), 0, 1024, dtype=jnp.int32)
    nsa_w = NSA_HEADS * NSA_HEAD_DIM
    mla_w = MLA_HEADS * MLA_V_DIM
    return {
        'x': nrm(ks[0], (BATCH, SEQ, D), 1.0),
        'c': nrm(ks[1], (BATCH, D), 1.0),
        'positions': offset + jnp.arange(SEQ, dtype=jnp.int32)[None, :],
        'ada_w': nrm(ks[3], (L, D, 6 * D), 0.5 * D ** -0.5),
        'ada_b': nrm(ks[4], (L, 6 * D), 0.02),
        'attn_pre_g': gain(ks[5], (L, D)),
        'attn_post_g': gain(ks[6], (L, D)),
        'w_in': nrm(ks[7], (L, D, IN_COLS), D ** -0.5),
        'cmp_pe': nrm(ks[8], (L, 2, CMP_BLOCK, NSA_HEAD_DIM), 0.1),
        'cmp_w1': nrm(ks[9], (L, 2, CMP_BLOCK * NSA_HEAD_DIM, CMP_HIDDEN), (CMP_BLOCK * NSA_HEAD_DIM) ** -0.5),
        'cmp_b1': nrm(ks[10], (L, 2, CMP_HIDDEN), 0.02),
        'cmp_w2': nrm(ks[11], (L, 2, CMP_HIDDEN, NSA_HEAD_DIM), CMP_HIDDEN ** -0.5),
        'mla_q_norm_g': gain(ks[12], (L, MLA_Q_RANK)),
        'mla_w_q_up': nrm(ks[13], (L, MLA_Q_RANK, MLA_HEADS * (MLA_NOPE_DIM + MLA_ROPE_DIM)), MLA_Q_RANK ** -0.5),
        'mla_kv_norm_g': gain(ks[14], (L, MLA_KV_RANK)),
        'mla_w_kv_up': nrm(ks[15], (L, MLA_KV_RANK, MLA_HEADS * (MLA_NOPE_DIM + MLA_V_DIM)), MLA_KV_RANK ** -0.5),
        'w_branch_nsa': nrm(ks[16], (L, nsa_w, D), nsa_w ** -0.5),
        'w_branch_mla': nrm(ks[17], (L, mla_w, D), mla_w ** -0.5),
        'w_out': nrm(ks[18], (L, D, D), D ** -0.5),
        'ffn_pre_g': gain(ks[19], (L, D)),
        'ffn_post_g': gain(ks[20], (L, D)),
        'peer_w_q': nrm(ks[21], (L, D, PEER_HEADS * PEER_QUERY_DIM), D ** -0.5),
        'peer_sub_keys': nrm(ks[22], (L, PEER_HEADS, 2, PEER_N_KEYS, PEER_QUERY_DIM // 2), (PEER_QUERY_DIM // 2) ** -0.5),
        'peer_u': nrm(ks[23], (L, PEER_N_EXPERTS, D), D ** -0.5),
        'peer_v': nrm(ks[24], (L, PEER_N_EXPERTS, D), D ** -0.5),
    }

def reference(x, c, positions, ada_w, ada_b, attn_pre_g, attn_post_g, w_in, cmp_pe, cmp_w1, cmp_b1,
              cmp_w2, mla_q_norm_g, mla_w_q_up, mla_kv_norm_g, mla_w_kv_up, w_branch_nsa, w_branch_mla,
              w_out, ffn_pre_g, ffn_post_g, peer_w_q, peer_sub_keys, peer_u, peer_v):
    for l in range(DEPTH):
        mod = jax.nn.silu(c) @ ada_w[l] + ada_b[l]
        sh_a, sc_a, g_a, sh_f, sc_f, g_f = [m[:, None, :] for m in jnp.split(mod, 6, axis=-1)]
        h = rms_norm(x, attn_pre_g[l]) * (1 + sc_a) + sh_a
        y = token_mixer(h, positions, w_in[l], cmp_pe[l], cmp_w1[l], cmp_b1[l], cmp_w2[l],
                        mla_q_norm_g[l], mla_w_q_up[l], mla_kv_norm_g[l], mla_w_kv_up[l],
                        w_branch_nsa[l], w_branch_mla[l], w_out[l])
        x = x + g_a * rms_norm(y, attn_post_g[l])
        h = rms_norm(x, ffn_pre_g[l]) * (1 + sc_f) + sh_f
        y = peer_ffn(h, peer_w_q[l], peer_sub_keys[l], peer_u[l], peer_v[l])
        x = x + g_f * rms_norm(y, ffn_post_g[l])
    return x


_drawn_inputs = setup_inputs


def setup_inputs(seed=0):
    import zlib

    import numpy as np

    out = dict(_drawn_inputs(seed))
    spreads = {}
    factors = {'attn_pre_g': 3.453,
     'attn_post_g': 3.31,
     'cmp_b1': 2.934,
     'mla_q_norm_g': 6.545,
     'mla_kv_norm_g': 4.095,
     'ffn_post_g': 8.0}
    for name, (base, spread) in spreads.items():
        noise = np.random.default_rng([zlib.crc32(name.encode()), seed]).standard_normal(out[name].shape)
        drawn = base * np.exp(spread * noise) if base else spread * noise
        out[name] = jnp.asarray(drawn.astype(out[name].dtype))
    for name, factor in factors.items():
        out[name] = (out[name] * factor).astype(out[name].dtype)
    return out
```

```python
from contextlib import ExitStack

import numpy as np
import concourse.bass as bass
from concourse import mybir

ALU = mybir.AluOpType
ACT = mybir.ActivationFunctionType
AX_X = mybir.AxisListType.X
F32 = mybir.dt.float32
I32 = mybir.dt.int32
U32 = mybir.dt.uint32

P = 128
D = 2048
SEQ = 256
NT = SEQ // P
KD = D // P
NC = 512

HEADS, GROUPS, HD = 16, 4, 64
RPG = HEADS // GROUPS
NROPE, MROPE = 16, 32
CB, CS, CH = 32, 16, 256
NCMP = (SEQ - CB) // CS + 1
MQ, MKV, MN = 512, 256, 64
MD = MN + MROPE
Q0 = 0
KV0 = Q0 + HEADS * HD
G0 = KV0 + 3 * 2 * GROUPS * HD
CQ0 = G0 + 3 * HEADS
CKV0 = CQ0 + MQ
KR0 = CKV0 + MKV
GM0 = KR0 + MROPE
EPS = 1e-6
NEG = -1e30
NSA_SCALE = HD ** -0.5
MLA_SCALE = MD ** -0.5

PH, NK, TOPK = 8, 128, 16
RING = 8
BATCH = 4

WSLOTS = 8
ADA_SLOTS = 4
NSEG = 6

TWO_PI = 2.0 * np.pi
PI_PARTS = (6.28125, 0.0019340515136718750, 1.2556659146e-06)
MAGIC = 12582912.0
PI_CLAMP = 3.1415925


class Chain:

    def __init__(self, eng, sem):
        self.eng, self.sem, self.n, self.i, self.step = eng, sem, 0, None, 0

    def did(self, ins):
        ins.then_inc(self.sem, 1)
        self.n += 1
        return ins

    def wait(self):
        self.eng.wait_ge(self.sem, self.n if self.i is None else self.i * self.step + self.n)

    def link(self, ins):
        self.did(ins)
        self.wait()

    def enter(self, i, step):
        self.i, self.step, self.n0 = i, step, self.n

    def leave(self, times):
        assert self.n - self.n0 == self.step, (self.n - self.n0, self.step)
        self.n, self.i = self.n0 + times * self.step, None


def build(nc, x, c, positions, ada_w, ada_b, attn_pre_g, attn_post_g, w_in, cmp_pe, cmp_w1, cmp_b1, cmp_w2,
          mla_q_norm_g, mla_w_q_up, mla_kv_norm_g, mla_w_kv_up, w_branch_nsa, w_branch_mla, w_out,
          ffn_pre_g, ffn_post_g, peer_w_q, peer_sub_keys, peer_u, peer_v, out):
    mod_dram = nc.dram_tensor("mod_rows", [4, D], F32).ap()

    x_v = x.rearrange("o (t p) d -> p (o t) d", p=P)
    out_v = out.rearrange("o (t p) d -> p (o t) d", p=P)
    ada_v = ada_w.rearrange("l (p j) n -> p (l j) n", p=P)
    def rows(w):
        return w.rearrange("l (j p) n -> p (l j) n", p=P)
    win_v, qup_v, kvup_v = rows(w_in), rows(mla_w_q_up), rows(mla_w_kv_up)
    wn_v, wm_v, wo_v, wpq_v = rows(w_branch_nsa), rows(w_branch_mla), rows(w_out), rows(peer_w_q)
    w1_v = cmp_w1.rearrange("l s (j p) n -> p (l s) j n", p=P)
    u_tab = peer_u.rearrange("l e d -> (l e) d")
    v_tab = peer_v.rearrange("l e d -> (l e) d")

    with ExitStack() as ctx:
        def sem(name):
            return ctx.enter_context(nc.semaphore(name))

        KW = 256
        XR, WR, PR, GR, TR, AR, RR = 16, 32, 27, 32, 16, 36, 24
        WORK = 17
        total = XR + WR + PR + GR + TR + AR + RR + WORK
        arena = ctx.enter_context(nc.sbuf_tensor("arena", [P, total * KW], F32))
        o_x = 0
        o_w = o_x + XR * KW
        o_p = o_w + WR * KW
        o_g = o_p + PR * KW
        o_t = o_g + GR * KW
        o_a = o_t + TR * KW
        o_r = o_a + AR * KW
        o_k = o_r + RR * KW

        def at(off, *dims):
            n = int(np.prod(dims))
            v = arena[:, off:off + n]
            names = ["a", "b", "c", "d", "e"][:len(dims)]
            if len(dims) > 1:
                v = v.rearrange("p (" + " ".join(names) + ") -> p " + " ".join(names), **dict(zip(names, dims)))
            return v

        X = at(o_x, NT, D)
        wring = at(o_w, WSLOTS, 2, NC)
        w1ring = at(o_w, WSLOTS, 4, CH)
        proj = at(o_p, NT, GM0)
        gates = at(o_g, NT, 2, D)
        h_tok = at(o_g, NT, D)
        hT = at(o_t, KD, SEQ)
        ada_acc = [at(o_k, D), at(o_r, D)]
        ada_ring = at(o_a, ADA_SLOTS, D)
        shift_row = at(o_r, D)
        scale_row = at(o_r + 8 * KW, D)
        gain_row = at(o_r + 16 * KW, D)
        mod_row = at(o_r + 16 * KW, D)
        KT2 = at(o_t, 2, GROUPS, SEQ)
        cmpX = at(o_t + 8 * KW, 2, CB // 2, GROUPS * NCMP)
        qm = at(o_a, NT, HEADS * MD)
        kvm = at(o_a + 12 * KW, NT, HEADS * 2 * MN)
        cqT = at(o_a + 28 * KW, 4, SEQ)
        ckvT = at(o_a + 32 * KW, 2, SEQ)
        kdup = at(o_r, 2, NT, GROUPS, 2, HD)
        cmpHrep = at(o_r + 8 * KW, 2, GROUPS, 4, 32)
        cmpH = at(o_r + 12 * KW, 2, 2, GROUPS * NCMP)
        Pc = at(o_r + 13 * KW, NT, RPG, 32)
        PcT = at(o_r + 14 * KW, NT, P)
        ogrp = at(o_r + 15 * KW, NT, 8, HD)
        s_prob = at(o_r + 19 * KW, 2, 384)
        vcg = at(o_r + 22 * KW, RPG, HD)
        o_nsa = at(o_t, NT, HEADS * HD)
        o_mla = at(o_t + 8 * KW, NT, HEADS * HD)
        qst = at(o_k, NT, RPG * HD)
        kst = at(o_k + 2 * KW, 2, NT, 2, HD)
        qT = at(o_k + 4 * KW, 2, NT, P)
        kT = at(o_k + 6 * KW, 2, SEQ)
        mst = at(o_k, 2, 2, NT, MD)
        mT = at(o_k + 3 * KW, 2, 4, P)
        probT = at(o_k + 8 * KW, 2, 384)
        ropeT = at(o_r + 8 * KW, 4, NT, HEADS, 8)
        qg_row = at(o_k + 11 * KW, MQ)
        kvg_row = at(o_k + 13 * KW, MKV)
        w2k = at(o_k + 14 * KW, 2, 2, HD)
        w2v = at(o_k + 15 * KW, 2, HD)
        vc = at(o_k + 15 * KW + KW // 2, GROUPS, HD)
        oT = at(o_a, 16, SEQ)
        y = at(o_a + 16 * KW, NT, D)
        bias_tmp = at(o_k + 8 * KW, D)
        gain_tmp = at(o_p + 16 * KW, D)
        merged = at(o_p, NT, D)
        mergedT = at(o_t, KD, SEQ)
        gate_a_row = at(o_r, D)
        shift_f_row = at(o_r + 8 * KW, D)
        scale_f_row = at(o_r + 16 * KW, D)
        mtmp = at(o_k, 2, 2, NC)
        h2 = at(o_g, NT, D)
        qryT = at(o_g + 16 * KW, 2 * PH, SEQ)
        sk_raw = at(o_p, 2 * PH, P)
        skT = at(o_p + 8 * KW, 2 * PH, NK)
        scores = at(o_a, NT, PH, 2 * NK)
        yacc = at(o_a + 16 * KW, D)
        gate_f_row = at(o_a + 24 * KW, D)
        sst = at(o_a + 32 * KW, 2, NK)
        stmp = at(o_a + 33 * KW, 2 * NK)
        cand = at(o_a + 32 * KW, TOPK, TOPK)
        onehot = at(o_a + 34 * KW, 2, TOPK, TOPK)
        diag = [at(o, P) for o in [o_p + 24 * KW + P * i for i in range(6)] + [o_k + 16 * KW + P * i for i in range(2)]]
        slot_off = ([o_w + 8 * KW * i for i in range(4)] + [o_p + 8 * KW * i for i in range(3)]
                    + [o_g + (16 + 8 * i) * KW for i in range(2)] + [o_t + 8 * KW * i for i in range(2)]
                    + [o_r + 8 * KW * i for i in range(3)] + [o_k + 8 * KW * i for i in range(2)])
        Urow = [at(o, D) for o in slot_off[:RING]]
        Vrow = [at(o, D) for o in slot_off[RING:2 * RING]]

        def sb(name, shape, dt=F32):
            return ctx.enter_context(nc.sbuf_tensor(name, shape, dt))

        ident = sb("ident", [P, P])
        ones = sb("ones", [P, P])
        zeros = ones[:, :]
        causal = sb("causal", [P, 2 * P])
        blocks = sb("blocks", [P, RPG])
        cmask = sb("cmask", [P, NT, NCMP])
        cmask01 = sb("cmask01", [P, NT, NCMP])
        sincos = sb("sincos", [P, 2, NT, 16])
        ang = sb("ang", [P, 3, NT * 16])
        freq = sb("freq", [P, 16])
        pos_i = sb("pos_i", [P, NT], I32)
        pos_f = sb("pos_f", [P, NT])
        ccol = sb("ccol", [P, KD])
        csil = sb("csil", [P, KD])
        msq = sb("msq", [P, 16])
        rstd = sb("rstd", [P, 16])
        cmp_rows = sb("cmp_rows", [36, P])
        cmp_cols = sb("cmp_cols", [P, 36])
        kcT = sb("kcT", [P, GROUPS, NCMP])
        kcg = sb("kcg", [P, NCMP])
        gnsa = sb("gnsa", [P, NT, 3 * HEADS])
        gst = sb("gst", [P, NT, RPG * 3])
        csc = sb("csc", [P, 8, NCMP])
        cstat = sb("cstat", [P, 4, 8])
        smax = sb("smax", [P, 2, NT])
        nmax = sb("nmax", [P, 2, NT])
        ssum = sb("ssum", [P, 4, NT])
        srec = sb("srec", [P, 2, NT])
        top = sb("top", [P, 3, TOPK])
        topi = sb("topi", [P, 3, TOPK], U32)
        topf = sb("topf", [P, 2, TOPK])
        ab_u = sb("ab_u", [P, 2, TOPK], U32)
        ab_f = sb("ab_f", [P, 2, TOPK])
        i12 = sb("i12", [P, 2, TOPK])
        iota_i = sb("iota_i", [P, TOPK], I32)
        iota_f = sb("iota_f", [P, TOPK])
        exp_f = sb("exp_f", [P, TOPK])
        idx_next = sb("idx_next", [P, TOPK], U32)
        idx_now = sb("idx_now", [P, 2, TOPK], U32)
        gate_e = sb("gate_e", [P, TOPK])
        gate_s = sb("gate_s", [P, 4])
        gate_next = sb("gate_next", [P, TOPK])
        gate_now = sb("gate_now", [P, TOPK])
        dots = sb("dots", [P, TOPK])
        act_g = sb("act_g", [P, TOPK])
        coef = sb("coef", [P, TOPK])

        PS = ctx.enter_context(nc.psum_tensor("PS", [P, 8, 512], F32))

        dve_done, act_done, pool_done = sem("dve_done"), sem("act_done"), sem("pool_done")
        dve_passed, pool_passed = sem("dve_passed"), sem("pool_passed")
        x_in, small_in, consts = sem("x_in"), sem("small_in"), sem("consts")
        ada_in = [sem(f"ada_in{i}") for i in range(ADA_SLOTS)]
        ada_used, ada_cols, ada_taken = sem("ada_used"), sem("ada_cols"), sem("ada_taken")
        mod_ready, mod_stored = sem("mod_ready"), sem("mod_stored")
        w_landed = [sem(f"w_landed{i}") for i in range(WSLOTS)]
        w_used = sem("w_used")
        msq_ready, root_ready = sem("msq_ready"), sem("root_ready")
        angle_ready, sin_ready, silu_ready = sem("angle_ready"), sem("sin_ready"), sem("silu_ready")
        htok_ready = sem("htok_ready")
        tr_done = sem("tr_done")
        tr_out = [sem("tr_out_act"), sem("tr_out_dve")]
        pj_out = sem("pj_out")
        gnsa_ready = sem("gnsa_ready")
        rope_ready, kdup_ready, kt2_in, kt2_ready, cmpx_ready = (sem("rope_ready"), sem("kdup_ready"), sem("kt2_in"),
                                                                 sem("kt2_ready"), sem("cmpx_ready"))
        cmph_ready, cmprep_ready, cmpkv_in, cmpkv_ready = (
            sem("cmph_ready"), sem("cmprep_ready"), sem("cmpkv_in"), sem("cmpkv_ready"))
        lat_ready, qm_roped = sem("lat_ready"), sem("qm_roped")
        staged = sem("staged")
        heads_in, qT_ready, kT_ready = sem("heads_in"), sem("qT_ready"), sem("kT_ready")
        csc_in, cexp_in, cexp_ready, cprob_ready, pct_in, pct_ready, oc_in = (
            sem("csc_in"), sem("cexp_in"), sem("cexp_ready"), sem("cprob_ready"), sem("pct_in"), sem("pct_ready"),
            sem("oc_in"))
        s_in, s_free, prob_in, prob_ready, pt_in, pt_ready, o_in, o_free = (
            sem("s_in"), sem("s_free"), sem("prob_in"), sem("prob_ready"), sem("pt_in"), sem("pt_ready"),
            sem("o_in"), sem("o_free"))
        grp_ready, grp_free = sem("grp_ready"), sem("grp_free")
        m_staged, mt_in, mt_ready = sem("m_staged"), sem("mt_in"), sem("mt_ready")
        row_in, row_used, rows_ready = sem("row_in"), sem("row_used"), sem("rows_ready")
        br_out, merged_ready = sem("br_out"), sem("merged_ready")
        h2_ready, sk_in = sem("h2_ready"), sem("sk_in")
        q_out, sc_in, sc_out = sem("q_out"), sem("sc_in"), sem("sc_out")
        sst_ready, top_ready, gexp_ready, idx_ready, idx_taken = (sem("sst_ready"), sem("top_ready"), sem("gexp_ready"),
                                                                  sem("idx_ready"), sem("idx_taken"))
        u_in = [sem(f"u_in{i}") for i in range(RING)]
        v_in = [sem(f"v_in{i}") for i in range(RING)]
        u_free, v_free = sem("u_free"), sem("v_free")
        gelu_ready, coef_ready, diag_ready, y_ready = sem("gelu_ready"), sem("coef_ready"), sem("diag_ready"), sem("y_ready")
        zeros_ready = sem("zeros_ready")
        out_ready, out_stored = sem("out_ready"), sem("out_stored")

        CH_MAIN, CH_TAIL, CH_GATE = 6, 1, 8
        CH_QUP, CH_KVUP = HEADS * MD // NC, HEADS * 2 * MN // NC
        TAIL = GM0 - CH_MAIN * NC
        N_QUP = CH_MAIN + CH_TAIL + CH_GATE
        N_KVUP = N_QUP + CH_QUP
        N_OUT = N_KVUP + CH_KVUP
        W_TAIL = CH_MAIN * 8
        W_GATE = W_TAIL + 8
        W_CMP = W_GATE + CH_GATE * 8
        W_QUP = W_CMP + 8
        W_KVUP = W_QUP + CH_QUP * 2
        W_BR = W_KVUP + CH_KVUP
        W_OUT = W_BR + 4 * 8
        W_PQ = W_OUT + 4 * 8
        TB_H, TB_CMP, TB_LAT, TB_O, TB_M, TB_SK, TB_H2 = 8, 1, 3, 8, 8, 4, 8
        NB_CMP = TB_H
        NB_LAT = NB_CMP + TB_CMP
        NB_O = NB_LAT + TB_LAT
        NB_M = NB_O + TB_O
        NB_SK = NB_M + TB_M
        NB_H2 = NB_SK + TB_SK
        NSA_UNITS = GROUPS * RPG * 2
        MLA_BODY = 8
        RMS_X, RMS_LAT, RMS_Y, RMS_X1, RMS_F = 0, 2, 6, 8, 10

        def banks_out(eng, n):
            eng.wait_ge(tr_out[0], (n + 1) // 2)
            if n // 2:
                eng.wait_ge(tr_out[1], n // 2)

        def oT_place(n):
            return 4 * (n // 2), n % 2

        def h_place(n):
            return 4 * (n % 4), n // 4

        block = ctx.enter_context(nc.Block())

        @block.sync
        def _(sp):
            for t in range(NT):
                sp.dma_start(X[:, t, :], x_v[:, t, :]).then_inc(x_in, 16)

            def load(m, src, cols=NC, first=False, i=None, step=0):
                if not first:
                    need = m - WSLOTS + 1
                    sp.wait_ge(w_used, need if i is None else i * step + need)
                sp.dma_start(wring[:, m % WSLOTS, :, 0:cols], src).then_inc(w_landed[m % WSLOTS], 16)

            for k in range(8):
                load(k, win_v[:, 2 * k:2 * k + 2, 0:NC], first=True)
            with sp.Fori(0, CH_MAIN - 1) as i:
                for k in range(8):
                    load(8 + k, win_v[:, 2 * k:2 * k + 2, bass.ds(i * NC + NC, NC)], i=i, step=8)
            for k in range(8):
                load(W_TAIL + k, win_v[:, 2 * k:2 * k + 2, CH_MAIN * NC:GM0], cols=TAIL)
            with sp.Fori(0, CH_GATE) as i:
                for k in range(8):
                    load(W_GATE + k, win_v[:, 2 * k:2 * k + 2, bass.ds(i * NC + GM0, NC)], i=i, step=8)
            for k in range(8):
                sp.wait_ge(w_used, W_CMP + k - WSLOTS + 1)
                sp.dma_start(w1ring[:, (W_CMP + k) % WSLOTS, :, :],
                             w1_v[:, k // 4, 4 * (k % 4):4 * (k % 4) + 4, :]).then_inc(w_landed[(W_CMP + k) % WSLOTS], 16)
            for n in range(CH_QUP):
                for k in range(2):
                    load(W_QUP + 2 * n + k, qup_v[:, 2 * k:2 * k + 2, n * NC:(n + 1) * NC])
            for n in range(CH_KVUP):
                load(W_KVUP + n, kvup_v[:, 0:2, n * NC:(n + 1) * NC])
            sp.wait_ge(mod_stored, 16 * 5)
            sp.wait_ge(o_free, 2 + NSA_UNITS + HEADS)
            sp.wait_ge(grp_free, 1 + GROUPS + HEADS // MLA_BODY)
            for dst, row, seg, gain in ((gate_a_row, 0, 2, attn_post_g), (shift_f_row, 1, 3, None),
                                        (scale_f_row, 2, 4, ffn_pre_g)):
                if row:
                    sp.wait_ge(row_used, row)
                sp.dma_start(dst, mod_dram[row, :].partition_broadcast(P)).then_inc(row_in, 16)
                sp.dma_start(bias_tmp, ada_b[0, seg * D:(seg + 1) * D].partition_broadcast(P)).then_inc(row_in, 16)
                if gain is not None:
                    sp.dma_start(gain_tmp, gain[0, :].partition_broadcast(P)).then_inc(row_in, 16)
            with sp.Fori(0, 4) as i:
                for k in range(8):
                    w_v = wn_v if k < 4 else wm_v
                    kk = 2 * (k % 4)
                    load(W_BR + k, w_v[:, kk:kk + 2, bass.ds(i * NC, NC)], i=i, step=8)
            for w0, w_v in ((W_OUT, wo_v), (W_PQ, wpq_v)):
                with sp.Fori(0, 4) as i:
                    for k in range(8):
                        load(w0 + k, w_v[:, 2 * k:2 * k + 2, bass.ds(i * NC, NC)], i=i, step=8)
                if w0 == W_OUT:
                    banks_out(sp, NB_M + TB_M)
                    sk_v = peer_sub_keys.rearrange("l h s n d -> (l h s) n d")
                    for k in range(2 * PH):
                        sp.dma_start(sk_raw[:, k, :], sk_v[k]).then_inc(sk_in, 16)
            sp.wait_ge(h2_ready, NT)
            sp.dma_start(gate_f_row, mod_dram[3, :].partition_broadcast(P)).then_inc(row_in, 16)
            sp.dma_start(bias_tmp, ada_b[0, 5 * D:6 * D].partition_broadcast(P)).then_inc(row_in, 16)
            sp.dma_start(yacc, ffn_post_g[0, :].partition_broadcast(P)).then_inc(row_in, 16)
            for t in range(NT):
                sp.wait_ge(out_ready, t + 1)
                sp.dma_start(out_v[:, t, :], X[:, t, :]).then_inc(out_stored, 16)
            sp.wait_ge(out_stored, 16 * NT)

        @block.gpsimd
        def _(pool):
            ch = Chain(pool, pool_done)
            def ada(j, seg, i=None):
                n = seg * KD + j
                if i is None:
                    src = ada_v[:, j, seg * D:(seg + 1) * D]
                    if n >= ADA_SLOTS:
                        pool.wait_ge(ada_used, n - ADA_SLOTS + 1)
                else:
                    src = ada_v[:, j, bass.ds(i * D + seg * D, D)]
                    pool.wait_ge(ada_used, i * KD + (n - ADA_SLOTS + 1))
                pool.dma_start(ada_ring[:, j % ADA_SLOTS, :], src).then_inc(ada_in[j % ADA_SLOTS], 16)
            for j in range(ADA_SLOTS):
                ada(j, 0)
            pool.memset(ident[:, :], 0.0).then_inc(pool_done, 1)
            pool.memset(ones[:, :], 1.0).then_inc(pool_done, 1)
            pool.memset(causal[:, :], 0.0).then_inc(pool_done, 1)
            pool.memset(cmask[:, :, :], 0.0).then_inc(pool_done, 1)
            pool.memset(cmask01[:, :, :], 1.0).then_inc(pool_done, 1)
            ch.n = 5
            ch.wait()
            pool.affine_select(out=ident[:, :], in_=ident[:, :], compare_op=ALU.not_equal, fill=1.0, base=0,
                               pattern=[[-1, P]], channel_multiplier=1).then_inc(consts, 1)
            pool.affine_select(out=causal[:, P:2 * P], in_=causal[:, P:2 * P], compare_op=ALU.is_ge, fill=NEG, base=0,
                               pattern=[[-1, P]], channel_multiplier=1).then_inc(consts, 1)
            for t in range(NT):
                pool.affine_select(out=cmask[:, t, :], in_=cmask[:, t, :], compare_op=ALU.is_ge, fill=NEG,
                                   base=t * P - CB + 1, pattern=[[-CS, NCMP]], channel_multiplier=1).then_inc(consts, 1)
                pool.affine_select(out=cmask01[:, t, :], in_=cmask01[:, t, :], compare_op=ALU.is_ge, fill=0.0,
                                   base=t * P - CB + 1, pattern=[[-CS, NCMP]], channel_multiplier=1).then_inc(consts, 1)
            pool.memset(blocks[:, :], 1.0).then_inc(pool_done, 1)
            pool.wait_ge(pool_done, 6)
            pool.affine_select(out=blocks[:, :], in_=blocks[:, :], compare_op=ALU.is_ge, fill=0.0, base=0,
                               pattern=[[-32, RPG]], channel_multiplier=1).then_inc(pool_done, 1)
            pool.wait_ge(pool_done, 7)
            pool.affine_select(out=blocks[:, :], in_=blocks[:, :], compare_op=ALU.is_ge, fill=0.0, base=31,
                               pattern=[[32, RPG]], channel_multiplier=-1).then_inc(pool_done, 1)
            pool.iota(iota_i[:, :], pattern=[[1, TOPK]], base=0, channel_multiplier=0).then_inc(consts, 1)
            for j in range(ADA_SLOTS, KD):
                ada(j, 0)
            with pool.Fori(0, NSEG - 1) as i:
                for j in range(KD):
                    ada(j, 1, i)

            pool.wait_ge(rope_ready, 1)
            pool.wait_ge(ada_cols, NSEG)
            pool.wait_ge(pj_out, 2 + CH_MAIN)
            for s in range(2):
                for t in range(NT):
                    src = proj[:, t, KV0 + s * GROUPS * HD:KV0 + (s + 1) * GROUPS * HD]
                    src = src.rearrange("p (g d) -> p g d", g=GROUPS)
                    for copy in range(2):
                        pool.tensor_copy(kdup[:, s, t, :, copy, :], src).then_inc(kdup_ready, 1)

            pool.wait_ge(gnsa_ready, 1)
            pool.wait_ge(cmpkv_ready, 2)
            pool.wait_ge(mod_stored, 16 * 5)
            with pool.Fori(0, GROUPS) as g:
                pool.tensor_copy(qst, proj[:, :, bass.ds(g * (RPG * HD) + Q0, RPG * HD)]).then_inc(staged, 1)
                for b in range(2):
                    src = proj[:, :, bass.ds(g * HD + (KV0 + (b + 1) * 2 * GROUPS * HD), HD)]
                    for copy in range(2):
                        pool.tensor_copy(kst[:, b, :, copy, :], src).then_inc(staged, 1)
                pool.tensor_copy(kcg[:, :], kcT[:, g, :]).then_inc(staged, 1)
                pool.tensor_tensor(vcg, vc[:, bass.ds(g, 1), :].to_broadcast([P, RPG, HD]),
                                   blocks[:, :].unsqueeze(2).to_broadcast([P, RPG, HD]), ALU.mult).then_inc(staged, 1)
                pool.tensor_copy(gst[:, :, :], gnsa[:, :, bass.ds(g * (RPG * 3), RPG * 3)]).then_inc(staged, 1)
                pool.wait_ge(grp_ready, g + 1)
                pool.tensor_copy(o_nsa[:, :, bass.ds(g * (RPG * HD), RPG * HD)].rearrange("p t (r d) -> p t r d", d=HD),
                                 ogrp[:, :, 0:RPG, :]).then_inc(grp_free, 1)

            pool.wait_ge(qm_roped, 1)
            pool.wait_ge(s_in, NSA_UNITS)
            with pool.Fori(0, HEADS // MLA_BODY) as i:
                for r in range(MLA_BODY):
                    pool.wait_ge(mt_in, i * MLA_BODY + (r + 1))
                    qsrc = qm[:, :, bass.ds(i * (MLA_BODY * MD) + r * MD, MD)]
                    ksrc = kvm[:, :, bass.ds(i * (MLA_BODY * 2 * MN) + r * 2 * MN, MN)]
                    pool.tensor_copy(mst[:, r % 2, 0, :, :], qsrc).then_inc(m_staged, 1)
                    pool.tensor_copy(mst[:, r % 2, 1, :, 0:MN], ksrc).then_inc(m_staged, 1)
                    pool.tensor_copy(mst[:, r % 2, 1, :, MN:MD], proj[:, :, KR0:KR0 + MROPE]).then_inc(m_staged, 1)
                pool.wait_ge(grp_ready, i + (GROUPS + 1))
                pool.tensor_copy(o_mla[:, :, bass.ds(i * (MLA_BODY * HD), MLA_BODY * HD)].rearrange(
                    "p t (r d) -> p t r d", d=HD), ogrp[:, :, :, :]).then_inc(grp_free, 1)

            def unit(u, now):
                pool.wait_ge(idx_ready, u + 1)
                pool.sem_inc(pool_passed, 1)
                pool.tensor_copy(idx_now[:, now, :], idx_next[:, :]).then_inc(idx_taken, 1)
                pool.wait_ge(idx_taken, u + 2)
                pool.sem_inc(pool_passed, 1)
                for b in range(TOPK // BATCH):
                    for tab, ring, free, landed in ((u_tab, Urow, u_free, u_in), (v_tab, Vrow, v_free, v_in)):
                        pool.wait_ge(free, u * TOPK + (b + 1) * BATCH)
                        pool.sem_inc(pool_passed, 1)
                        for e in range(b * BATCH, (b + 1) * BATCH):
                            pool.indirect_dma_start(
                                ring[e % RING], None, tab,
                                bass.IndirectOffsetOnAxis(ap=idx_now[:, now, e:e + 1], axis=0)).then_inc(landed[e % RING], 16)
            pool.wait_ge(sc_out, 8)
            pool.wait_ge(h2_ready, NT)
            with pool.Fori(0, PH) as i:
                for k in range(2):
                    unit(i * 2 + k, k)

        @block.scalar
        def _(act):
            with nc.allow_non_contiguous_dma("a few hundred words"):
                act.dma_start(ccol[:, :], c.rearrange("o (p j) -> (o p) j", p=P)).then_inc(small_in, 16)
                act.dma_start(pos_i[:, :], positions.rearrange("o (t p) -> p (o t)", p=P)).then_inc(small_in, 16)
            act.dma_start(shift_row, ada_b[0, 0:D].partition_broadcast(P)).then_inc(small_in, 16)
            act.dma_start(scale_row, ada_b[0, D:2 * D].partition_broadcast(P)).then_inc(small_in, 16)
            act.dma_start(gain_row, attn_pre_g[0, :].partition_broadcast(P)).then_inc(small_in, 16)
            act.dma_start(qg_row[:, :], mla_q_norm_g[0, :].partition_broadcast(P)).then_inc(small_in, 16)
            act.dma_start(kvg_row[:, :], mla_kv_norm_g[0, :].partition_broadcast(P)).then_inc(small_in, 16)
            act.dma_start(cmp_rows[0:32, :], cmp_pe.rearrange("l s (i e) d -> (l s i) (e d)", e=2)).then_inc(small_in, 16)
            act.dma_start(cmp_rows[32:36, :], cmp_b1.rearrange("l s (h n) -> (l s h) n", n=P)).then_inc(small_in, 16)
            w2_v = cmp_w2.rearrange("l s (h p) d -> p (l s) h d", p=P)
            for copy in range(2):
                act.dma_start(w2k[:, :, copy, :], w2_v[:, 0, :, :]).then_inc(small_in, 16)
            act.dma_start(w2v[:, :, :], w2_v[:, 1, :, :]).then_inc(small_in, 16)
            act.wait_ge(small_in, 16 * 12)
            nc.scalar.activation(csil[:, :], ccol[:, :], ACT.Silu).then_inc(silu_ready, 1)
            act.wait_ge(angle_ready, 1)
            nc.scalar.activation(sincos[:, 0, :, :], ang[:, 0, :], ACT.Sin).then_inc(sin_ready, 1)
            nc.scalar.activation(sincos[:, 1, :, :], ang[:, 1, :], ACT.Sin).then_inc(sin_ready, 1)

            def root(n, col, cnt):
                act.wait_ge(msq_ready, n)
                nc.scalar.activation(rstd[:, col:col + cnt], msq[:, col:col + cnt], ACT.Sqrt).then_inc(root_ready, 1)

            def bank_out(n, dst, upto=4 * P):
                act.wait_ge(tr_done, n + 1)
                src = PS[:, 4 + n % 4, 0:upto]
                if len(dst.shape) == 3:
                    src = src.rearrange("p (a b) -> p a b", b=P)
                nc.scalar.copy(dst, src).then_inc(tr_out[0], 1)

            root(1, RMS_X, NT)
            for n in range(0, TB_H, 2):
                bank_out(n, hT[:, 4 * (n % 4):4 * (n % 4) + 4, (n // 4) * P:(n // 4 + 1) * P])

            def chunk_out(n, m_end, dst, func=ACT.Copy, i=None, step=0, tiles=0):
                act.wait_ge(w_used, m_end if i is None else i * (step * tiles) + m_end)
                for t in range(NT):
                    d = dst(t)
                    ins = nc.scalar.activation(d, PS[:, (n % 2) * 2 + t, 0:d.shape[-1]], func)
                ins.then_inc(pj_out, 1)

            def mod_out(r, i):
                act.wait_ge(ada_cols, i * 2 + (r + 3))
                act.wait_ge(mod_stored, i * 32 + 16 * (r + 1))
                nc.scalar.copy(mod_row[0:1, :].rearrange("p (a b) -> p a b", a=4), PS[0:1, 4:8, :]).then_inc(mod_ready, 1)
                act.wait_ge(mod_ready, i * 2 + (r + 2))
                act.dma_start(mod_dram[bass.ds(i * 2 + r, 1), :], mod_row[0:1, :]).then_inc(mod_stored, 16)

            with act.Fori(0, CH_MAIN // 2) as i:
                for k in range(2):
                    chunk_out(k, 8 * (k + 1), lambda t: proj[:, t, bass.ds(i * (2 * NC) + k * NC, NC)], ACT.Copy, i, 2, 8)
            chunk_out(CH_MAIN, W_GATE, lambda t: proj[:, t, CH_MAIN * NC:GM0])
            gates_v = gates.rearrange("p t s d -> p t (s d)")
            with act.Fori(0, 2) as i:
                for k in range(4):
                    chunk_out(CH_MAIN + 1 + k, W_GATE + 8 * (k + 1),
                              lambda t: gates_v[:, t, bass.ds(i * (4 * NC) + k * NC, NC)], ACT.Sigmoid, i, 4, 8)
                    if k % 2:
                        mod_out(k // 2, i)
            act.wait_ge(pj_out, 2 + CH_MAIN)
            nc.scalar.activation(gnsa[:, :, :], proj[:, :, G0:CQ0], ACT.Sigmoid).then_inc(gnsa_ready, 1)

            act.wait_ge(tr_done, NB_CMP + 1)
            nc.scalar.copy(cmp_cols[:, :], PS[:, 4 + NB_CMP % 4, 0:36]).then_inc(tr_out[0], 1)
            root(2, RMS_LAT, 4)
            bank_out(NB_LAT + 1, cqT[:, :, P:2 * P])
            for b in range(4):
                act.wait_ge(kt2_in, b + 1)
                nc.scalar.copy(KT2[HD:P, b // 2, 2 * (b % 2):2 * (b % 2) + 2, 0:SEQ - 1],
                               PS[HD:P, b, :].rearrange("p (g t) -> p g t", g=2)[:, :, 1:SEQ]).then_inc(kt2_ready, 1)
            act.wait_ge(tr_out[0], NB_CMP // 2 + 1)
            for s in range(2):
                act.wait_ge(w_used, W_CMP + 4 * (s + 1))
                for h in range(2):
                    ins = nc.scalar.activation(cmpH[:, s, h, :], PS[:, 2 * s + h, 0:GROUPS * NCMP], ACT.Gelu_apprx_tanh,
                                               bias=cmp_cols[:, 32 + 2 * s + h:33 + 2 * s + h])
                ins.then_inc(cmph_ready, 1)
            for k in range(CH_QUP):
                chunk_out(N_QUP + k, W_QUP + 2 * (k + 1), lambda t: qm[:, t, k * NC:(k + 1) * NC])
            for k in range(CH_KVUP):
                chunk_out(N_KVUP + k, W_KVUP + k + 1, lambda t: kvm[:, t, k * NC:(k + 1) * NC])

            def softmax_exp(n, i, step, scale):
                ring = n % 2
                act.wait_ge(prob_in, i * step + (n + 1))
                for t in range(NT):
                    lo, hi = (0, P) if t == 0 else (P, 3 * P)
                    ins = nc.scalar.activation(s_prob[:, ring, lo:hi], s_prob[:, ring, lo:hi], ACT.Exp,
                                               bias=nmax[:, ring, t:t + 1], scale=scale,
                                               accum_out=ssum[:, n % 4, t:t + 1])
                ins.then_inc(prob_ready, 1)

            def probs_out(n, i, step):
                act.wait_ge(o_in, i * step + (n + 1))
                act.wait_ge(pt_in, i * step + (n + 3))
                nc.scalar.copy(probT[:, n % 2, :], PS[:, 2 + n % 2, 0:384]).then_inc(pt_ready, 1)

            U = 2 * RPG
            with act.Fori(0, GROUPS) as g:
                act.wait_ge(heads_in, g * 2 + 1)
                nc.scalar.copy(qT.rearrange("p a t b -> p (a t b)"), PS[:, 6, :]).then_inc(qT_ready, 1)
                act.wait_ge(cexp_in, g + 1)
                nc.scalar.activation(csc[:, :, :], csc[:, :, :], ACT.Exp, scale=NSA_SCALE).then_inc(cexp_ready, 1)
                for n in range(U + 1):
                    if n < U:
                        softmax_exp(n, g, U, NSA_SCALE)
                    if n >= 1:
                        probs_out(n - 1, g, U)
            with act.Fori(0, HEADS // MLA_BODY) as i:
                for n in range(MLA_BODY + 1):
                    if n < MLA_BODY:
                        softmax_exp(NSA_UNITS + n, i, MLA_BODY, MLA_SCALE)
                    if n >= 1:
                        probs_out(NSA_UNITS + n - 1, i, MLA_BODY)

            for n in range(NB_O, NB_O + TB_O, 2):
                a, t = oT_place(n - NB_O)
                bank_out(n, oT[:, a:a + 4, t * P:(t + 1) * P])
            for n in range(NB_M, NB_M + TB_M, 2):
                a, t = h_place(n - NB_M)
                bank_out(n, mergedT[:, a:a + 4, t * P:(t + 1) * P])
            with act.Fori(0, 2) as i:
                for k in range(2):
                    chunk_out(N_OUT + k, W_OUT + 8 * (k + 1), lambda t: y[:, t, bass.ds(i * (2 * NC) + k * NC, NC)],
                              ACT.Copy, i, 2, 8)
            root(3, RMS_Y, NT)
            for n in range(NB_SK, NB_SK + TB_SK, 2):
                bank_out(n, skT[:, 4 * (n - NB_SK):4 * (n - NB_SK) + 4, :])
            root(4, RMS_X1, NT)
            for n in range(NB_H2, NB_H2 + TB_H2, 2):
                a, t = h_place(n - NB_H2)
                bank_out(n, hT[:, a:a + 4, t * P:(t + 1) * P])
            with act.Fori(0, 2) as i:
                for n in range(2):
                    act.wait_ge(w_used, i * 16 + (W_PQ + 8 * (n + 1)))
                    for k in range(4):
                        ins = nc.scalar.copy(qryT[:, bass.ds(i * 8 + 4 * n + k, 1), :].rearrange("p a t -> p (a t)"),
                                             PS[:, 4 * n + k, 0:SEQ])
                    ins.then_inc(q_out, 1)
            for n in range(8):
                act.wait_ge(sc_in, n + 1)
                nc.scalar.copy(scores[:, n // 4, 2 * (n % 4):2 * (n % 4) + 2, :],
                               PS[:, n, :].rearrange("p (h n) -> p h n", h=2)).then_inc(sc_out, 1)

            act.wait_ge(sc_out, 8)
            scores_v = scores.rearrange("p t h n -> p (t h) n")

            def fetch(src):
                nc.scalar.copy(sst.rearrange("p s n -> p (s n)"), src).then_inc(sst_ready, 1)

            def gate_exp(u):
                act.wait_ge(top_ready, u + 1)
                nc.scalar.activation(gate_e[:, :], top[:, 2, :], ACT.Exp, bias=gate_s[:, 0:1],
                                     accum_out=gate_s[:, 1:2]).then_inc(gexp_ready, 1)

            def unit(u, last=False):
                if not last:
                    act.wait_ge(idx_ready, u + 1)
                    fetch(scores_v[:, bass.ds(u + 1, 1), :].rearrange("p a n -> p (a n)"))
                for b in range(TOPK // BATCH):
                    cols = slice(b * BATCH, (b + 1) * BATCH)
                    act.wait_ge(u_free, u * TOPK + (RING + (b + 1) * BATCH))
                    nc.scalar.activation(act_g[:, cols], dots[:, cols], ACT.Gelu_apprx_tanh).then_inc(gelu_ready, 1)
                    if b == 2 and not last:
                        gate_exp(u + 1)
                    act.wait_ge(v_free, u * TOPK + (b + 1) * BATCH)
                    act.wait_ge(coef_ready, u * 4 + (b + 1))
                    for e in range(b * BATCH, (b + 1) * BATCH):
                        nc.scalar.activation(diag[e % 8], ident[:, :], ACT.Copy,
                                             scale=coef[:, e:e + 1]).then_inc(diag_ready, 1)

            def y_out(t):
                act.wait_ge(v_free, RING + (t + 1) * PH * TOPK)
                if t:
                    act.wait_ge(out_ready, t)
                nc.scalar.copy(yacc.rearrange("p (a b) -> p a b", a=4), PS[:, 4 * t:4 * t + 4, :]).then_inc(y_ready, 1)

            fetch(scores_v[:, 0, :])
            gate_exp(0)
            with act.Fori(0, PH) as u:
                unit(u)
            y_out(0)
            root(5, RMS_F, 1)
            with act.Fori(0, PH - 1) as u:
                unit(u + PH)
            unit(2 * PH - 1, True)
            y_out(1)
            root(6, RMS_F + 1, 1)

        @block.tensor
        def _(pe):
            def tile_ready(m, i=None, uses=0):
                v = 16 * (m // WSLOTS + 1)
                pe.wait_ge(w_landed[m % WSLOTS], v if i is None else i * (16 * uses) + v)

            def transposes(n, srcs):
                if n >= 4:
                    pe.wait_ge(tr_out[n % 2], n // 2 - 1)
                for k, s in enumerate(srcs):
                    r = s.shape[0]
                    ins = nc.tensor.transpose(PS[0:s.shape[1], 4 + n % 4, k * P:k * P + r], s, ident[0:r, 0:r])
                ins.then_inc(tr_done, 1)

            def column_sums(acc, m):
                for k in range(4):
                    ins = nc.tensor.matmul(PS[0:m, 4 + k, :], ones[:, 0:m], acc[:, k * NC:(k + 1) * NC],
                                           start=True, stop=True)
                ins.then_inc(ada_cols, 1)

            def chunk(n, m, lhs, ktiles, cols=NC, i=None, step=0):
                if i is not None:
                    pe.wait_ge(pj_out, i * step + (n - 1))
                elif n >= 2:
                    pe.wait_ge(pj_out, n - 1)
                for w in range(ktiles // 2):
                    tile_ready(m + w, i, step)
                    for k in range(2):
                        for t in range(NT):
                            kk = 2 * w + k
                            ins = nc.tensor.matmul(PS[:, (n % 2) * 2 + t, 0:cols], lhs[:, kk, t * P:(t + 1) * P],
                                                   wring[:, (m + w) % WSLOTS, k, 0:cols],
                                                   start=(kk == 0), stop=(kk == ktiles - 1))
                    ins.then_inc(w_used, 1)

            pe.wait_ge(consts, 7)
            pe.wait_ge(pool_done, 5)
            pe.wait_ge(ada_used, KD)
            column_sums(ada_acc[0], P)
            pe.wait_ge(ada_used, 2 * KD)
            pe.wait_ge(ada_taken, 1)
            column_sums(ada_acc[0], P)
            pe.wait_ge(ada_taken, 2)
            for n in range(TB_H):
                a, t = h_place(n)
                pe.wait_ge(htok_ready, t + 1)
                transposes(n, [h_tok[:, t, (a + k) * P:(a + k + 1) * P] for k in range(4)])
            banks_out(pe, TB_H)

            with pe.Fori(0, CH_MAIN // 2) as i:
                for k in range(2):
                    chunk(2 + k, 8 * k, hT, KD, i=i, step=2)
            chunk(2 + CH_MAIN, W_TAIL, hT, KD, cols=TAIL)
            with pe.Fori(0, 2) as i:
                for k in range(4):
                    chunk(2 + CH_MAIN + 1 + k, W_GATE + 8 * k, hT, KD, i=i, step=4)
                    if k % 2:
                        pe.wait_ge(ada_used, i * (2 * KD) + KD * (3 + k // 2))
                        pe.wait_ge(mod_ready, i * 2 + (k // 2 + 1))
                        column_sums(ada_acc[1 - k // 2], 1)

            pe.wait_ge(mod_ready, 5)
            transposes(NB_CMP, [cmp_rows[:, :]])
            pe.wait_ge(lat_ready, 1)
            for t in range(NT):
                transposes(NB_LAT + t, [proj[:, t, CQ0 + k * P:CQ0 + (k + 1) * P] for k in range(4)])
            transposes(NB_LAT + 2, [proj[:, t, CKV0 + k * P:CKV0 + (k + 1) * P] for k in range(2) for t in range(NT)])
            pe.wait_ge(pj_out, 2 + CH_MAIN + 1 + CH_GATE)
            pe.wait_ge(kdup_ready, 8)
            for b in range(4):
                for k in range(4):
                    g, t = 2 * (b % 2) + k // 2, k % 2
                    ins = nc.tensor.transpose(PS[:, b, k * P:(k + 1) * P],
                                              kdup[:, b // 2, t, g, :, :].rearrange("p a d -> p (a d)"), ident[:, :])
                ins.then_inc(kt2_in, 1)
            pe.wait_ge(kt2_ready, 4)
            for k in range(8):
                s = k // 4
                if k % 4 == 0:
                    pe.wait_ge(cmpx_ready, s + 1)
                tile_ready(W_CMP + k)
                for kk in range(4):
                    j = 4 * (k % 4) + kk
                    for h in range(2):
                        ins = nc.tensor.matmul(PS[:, 2 * s + h, 0:GROUPS * NCMP],
                                               w1ring[:, (W_CMP + k) % WSLOTS, kk, h * P:(h + 1) * P],
                                               cmpX[:, s, j, :], start=(j == 0), stop=(j == CB // 2 - 1))
                ins.then_inc(w_used, 1)
            pe.wait_ge(cmph_ready, 1)
            for h in range(2):
                ins = nc.tensor.matmul(PS[:, 0, 0:GROUPS * NCMP], w2k[:, h, :, :].rearrange("p a d -> p (a d)"),
                                       cmpH[:, 0, h, :], start=(h == 0), stop=(h == 1))
            ins.then_inc(cmpkv_in, 1)
            pe.wait_ge(cmprep_ready, 2)
            for g in range(GROUPS):
                for h in range(2):
                    ins = nc.tensor.matmul(PS[:, 2, g * HD:(g + 1) * HD],
                                           cmpHrep[:, h, g, :, :].rearrange("p a b -> p (a b)"), w2v[:, h, :],
                                           start=(h == 0), stop=(h == 1))
            ins.then_inc(cmpkv_in, 1)
            pe.wait_ge(cmpkv_ready, 2)
            banks_out(pe, NB_LAT + TB_LAT)
            for k in range(CH_QUP):
                chunk(2 + N_QUP + k, W_QUP + 2 * k, cqT, 4)
            for k in range(CH_KVUP):
                chunk(2 + N_KVUP + k, W_KVUP + k, ckvT, 2)

            def score(n, i, step, q, k):
                pe.wait_ge(s_free, i * step + (n + 1))
                nc.tensor.matmul(PS[:, n % 2, 0:P], q(0), k(0, P), start=True, stop=True)
                nc.tensor.matmul(PS[:, n % 2, P:3 * P], q(1), k(0, 2 * P), start=True, stop=True).then_inc(s_in, 1)

            def turn(n, i, step):
                pe.wait_ge(prob_ready, i * step + (n + 1))
                pe.wait_ge(pt_ready, i * step + (n + 1))
                for k in range(3):
                    ins = nc.tensor.transpose(PS[:, 2 + n % 2, k * P:(k + 1) * P], s_prob[:, n % 2, k * P:(k + 1) * P],
                                              ident[:, :])
                ins.then_inc(pt_in, 1)

            def weigh(n, i, step, v):
                pe.wait_ge(pt_ready, i * step + (n + 3))
                pe.wait_ge(o_free, i * step + (n + 1))
                nc.tensor.matmul(PS[:, 4 + n % 2, 0:HD], probT[:, n % 2, 0:P], v(0), start=True, stop=True)
                nc.tensor.matmul(PS[:, 4 + n % 2, HD:2 * HD], probT[:, n % 2, P:2 * P], v(0), start=True, stop=False)
                nc.tensor.matmul(PS[:, 4 + n % 2, HD:2 * HD], probT[:, n % 2, 2 * P:3 * P], v(1),
                                 start=False, stop=True).then_inc(o_in, 1)

            pe.wait_ge(pj_out, 2 + N_OUT)
            U = 2 * RPG
            with pe.Fori(0, GROUPS) as g:
                pe.wait_ge(staged, g * 8 + 8)
                for k in range(4):
                    ins = nc.tensor.transpose(PS[:, 6, k * P:(k + 1) * P], qst[:, k % 2, (k // 2) * P:(k // 2 + 1) * P],
                                              ident[:, :])
                ins.then_inc(heads_in, 1)
                for k in range(4):
                    ins = nc.tensor.transpose(PS[:, 7, k * P:(k + 1) * P],
                                              kst[:, k // 2, k % 2, :, :].rearrange("p a d -> p (a d)"), ident[:, :])
                ins.then_inc(heads_in, 1)
                pe.wait_ge(qT_ready, g + 1)
                pe.wait_ge(kT_ready, g + 1)
                for t in range(NT):
                    for r in range(RPG):
                        half = slice(HD * (r % 2), HD * (r % 2) + HD)
                        ins = nc.tensor.matmul(PS[:, 7 - r % 2, (t * RPG + r) * 16:(t * RPG + r) * 16 + NCMP],
                                               qT[half, r // 2, t, :], kcg[half, :], start=True, stop=True)
                        if t == NT - 1 and r >= RPG - 2:
                            ins.then_inc(csc_in, 1)
                for n in range(U + 2):
                    if n < U:
                        r, b = n // 2, n % 2
                        half = slice(HD * (r % 2), HD * (r % 2) + HD)
                        score(n, g, U, lambda t: qT[half, r // 2, t, :], lambda lo, hi: kT[half, b, lo:hi])
                    if n == 1:
                        pe.wait_ge(cprob_ready, g + 1)
                        for t in range(NT):
                            ins = nc.tensor.transpose(PS[:, 6, t * P:(t + 1) * P],
                                                      Pc[:, t, :, :].rearrange("p r b -> p (r b)"), ident[:, :])
                        ins.then_inc(pct_in, 1)
                    if 1 <= n <= U:
                        turn(n - 1, g, U)
                    if n == 1:
                        pe.wait_ge(pct_ready, g + 1)
                        for t in range(NT):
                            ins = nc.tensor.matmul(PS[:, 7, t * RPG * HD:(t + 1) * RPG * HD], PcT[:, t, :],
                                                   vcg.rearrange("p r d -> p (r d)"), start=True, stop=True)
                        ins.then_inc(oc_in, 1)
                    if n >= 2:
                        b = (n - 2) % 2
                        weigh(n - 2, g, U, lambda kt: proj[:, kt, bass.ds(
                            g * HD + (KV0 + ((b + 1) * 2 + 1) * GROUPS * HD), HD)])

            M = MLA_BODY
            with pe.Fori(0, HEADS // M) as i:
                def turn_heads(r):
                    pe.wait_ge(m_staged, i * (3 * M) + 3 * (r + 1))
                    pe.wait_ge(mt_ready, i * M + (r + 1))
                    for k in range(4):
                        ins = nc.tensor.transpose(PS[0:MD, 6 + r % 2, k * P:(k + 1) * P], mst[:, r % 2, k // 2, k % 2, :],
                                                  ident[:, :])
                    ins.then_inc(mt_in, 1)
                turn_heads(0)
                for n in range(M + 2):
                    if n + 1 < M:
                        turn_heads(n + 1)
                    if n < M:
                        pe.wait_ge(mt_ready, i * M + (n + 3))
                        score(NSA_UNITS + n, i, M, lambda t: mT[0:MD, n % 2, t, :],
                              lambda lo, hi: mT[0:MD, n % 2, 2:4, :].rearrange("p a b -> p (a b)")[:, lo:hi])
                    if 1 <= n <= M:
                        turn(NSA_UNITS + n - 1, i, M)
                    if n >= 2:
                        weigh(NSA_UNITS + n - 2, i, M, lambda kt: kvm[:, kt, bass.ds(
                            i * (M * 2 * MN) + (n - 2) * 2 * MN + MN, MN)])

            pe.wait_ge(grp_free, 1 + GROUPS + HEADS // M)
            pe.wait_ge(o_free, 2 + NSA_UNITS + HEADS)
            for n in range(TB_O):
                a, t = oT_place(n)
                src, j = (o_nsa, a) if a < 8 else (o_mla, a - 8)
                transposes(NB_O + n, [src[:, t, (j + k) * P:(j + k + 1) * P] for k in range(4)])
            banks_out(pe, NB_O + TB_O)

            with pe.Fori(0, 2) as i:
                for c_ in range(2):
                    pe.wait_ge(br_out, i * 2 + (c_ + 1))
                    for w in range(8):
                        m = W_BR + 8 * c_ + w
                        tile_ready(m, i, 2)
                        for k in range(2):
                            for t in range(NT):
                                kk = 2 * (w % 4) + k
                                ins = nc.tensor.matmul(PS[:, 4 * c_ + 2 * t + w // 4, :],
                                                       oT[:, 2 * w + k, t * P:(t + 1) * P], wring[:, m % WSLOTS, k, :],
                                                       start=(kk == 0), stop=(kk == 7))
                        ins.then_inc(w_used, 1)
            pe.wait_ge(br_out, 2 + 4)
            pe.wait_ge(merged_ready, 1)
            for n in range(TB_M):
                a, t = h_place(n)
                transposes(NB_M + n, [merged[:, t, (a + k) * P:(a + k + 1) * P] for k in range(4)])
            banks_out(pe, NB_M + TB_M)
            with pe.Fori(0, 2) as i:
                for k in range(2):
                    chunk(2 + N_OUT + k, W_OUT + 8 * k, mergedT, KD, i=i, step=2)

            pe.wait_ge(sk_in, 16 * 2 * PH)
            for n in range(TB_SK):
                transposes(NB_SK + n, [sk_raw[:, 4 * n + k, :] for k in range(4)])
            for n in range(TB_H2):
                a, t = h_place(n)
                pe.wait_ge(h2_ready, t + 1)
                transposes(NB_H2 + n, [h2[:, t, (a + k) * P:(a + k + 1) * P] for k in range(4)])
            banks_out(pe, NB_H2 + TB_H2)
            pe.wait_ge(pj_out, 2 + N_OUT + 4)
            with pe.Fori(0, 2) as i:
                for n in range(2):
                    pe.wait_ge(q_out, i * 2 + (n + 1))
                    for w in range(8):
                        m = W_PQ + 8 * n + w
                        tile_ready(m, i, 2)
                        for k in range(2):
                            for blk in range(4):
                                kk = 2 * w + k
                                ins = nc.tensor.matmul(PS[:, 4 * n + blk, 0:SEQ],
                                                       wring[:, m % WSLOTS, k, blk * P:(blk + 1) * P], hT[:, kk, :],
                                                       start=(kk == 0), stop=(kk == KD - 1))
                        ins.then_inc(w_used, 1)
            pe.wait_ge(q_out, 2 + 4)
            for n in range(8):
                t = n // 4
                for k in range(4):
                    hp = 4 * (n % 4) + k
                    ins = nc.tensor.matmul(PS[:, n, k * NK:(k + 1) * NK], qryT[:, hp, t * P:(t + 1) * P], skT[:, hp, :],
                                           start=True, stop=True)
                ins.then_inc(sc_in, 1)
            pe.wait_ge(sc_out, 8)

            def unit(u, bank):
                for e in range(TOPK):
                    pe.wait_ge(v_in[e % RING], u * 32 + 16 * (e // RING + 1))
                    pe.wait_ge(diag_ready, u * TOPK + (e + 1))
                    for k in range(4):
                        ins = nc.tensor.matmul(PS[:, bank + k, :], diag[e % 8], Vrow[e % RING][:, k * NC:(k + 1) * NC],
                                               start=False, stop=False, skip_group_check=True)
                    ins.then_inc(v_free, 1)
            pe.wait_ge(zeros_ready, 1)
            for bank in range(8):
                nc.tensor.matmul(PS[:, bank, :], zeros, scores[:, 0, 0:2, :].rearrange("p h n -> p (h n)"),
                                 start=True, stop=True)
            for t in range(NT):
                with pe.Fori(0, PH) as u:
                    unit(u + t * PH, 4 * t)

        @block.vector
        def _(dve):
            v = nc.vector
            ch = Chain(dve, dve_done)
            link = ch.link

            for k, (s, n) in enumerate(((s_free, 2), (pt_in, 2), (o_in, 2), (o_free, 2), (pt_ready, 2), (mt_in, 2),
                                        (mt_ready, 2), (br_out, 2), (q_out, 2), (u_free, RING), (v_free, RING),
                                        (pj_out, 2), (mod_stored, 16), (mod_ready, 1))):
                v.memset(msq[:, k:k + 1], 0.0).then_inc(s, n)

            for k, s in enumerate((grp_free, idx_taken)):
                v.memset(rstd[:, k:k + 1], 0.0).then_inc(s, 1)

            def reduced(r, k):
                link(v.tensor_scalar(ang[:, 2, :], ang[:, k, :], 1.0 / TWO_PI, None, ALU.mult))
                link(v.tensor_scalar(ang[:, 2, :], ang[:, 2, :], MAGIC, None, ALU.add))
                link(v.tensor_scalar(ang[:, 2, :], ang[:, 2, :], MAGIC, None, ALU.subtract))
                for part in PI_PARTS:
                    link(v.scalar_tensor_tensor(out=ang[:, r, :], in0=ang[:, 2, :], scalar=-part, in1=ang[:, r, :],
                                                op0=ALU.mult, op1=ALU.add))

            for k in range(16):
                f = float(np.float32(500000.0) ** np.float32(-k * (2.0 / MROPE)))
                ins = v.memset(freq[:, k:k + 1], f)
            link(ins)
            dve.wait_ge(small_in, 16 * 12)
            link(v.tensor_copy(pos_f[:, :], pos_i[:, :]))
            for t in range(NT):
                ins = v.tensor_scalar(ang[:, 0, t * 16:(t + 1) * 16], freq[:, :], pos_f[:, t:t + 1], None, ALU.mult)
            link(ins)
            reduced(0, 0)
            link(v.tensor_scalar(ang[:, 1, :], ang[:, 0, :], float(np.pi / 2), None, ALU.add))
            link(v.tensor_scalar(ang[:, 2, :], ang[:, 1, :], float(np.pi), -float(TWO_PI), ALU.is_gt, ALU.mult))
            link(v.tensor_tensor(ang[:, 1, :], ang[:, 1, :], ang[:, 2, :], ALU.add))
            v.tensor_scalar(ang[:, 0:2, :], ang[:, 0:2, :], PI_CLAMP, -PI_CLAMP, ALU.min, ALU.max).then_inc(angle_ready, 1)

            def mean_square(col, src, junk):
                return v.tensor_tensor_reduce(junk, src, src, 1.0 / src.shape[-1], EPS, ALU.mult, ALU.add,
                                              msq[:, col:col + 1])

            def inverse_root(n, col, cnt):
                dve.wait_ge(root_ready, n)
                link(v.reciprocal(rstd[:, col:col + cnt], rstd[:, col:col + cnt]))

            dve.wait_ge(x_in, 16 * NT)
            ch.wait()
            for t in range(NT):
                ins = mean_square(RMS_X + t, X[:, t, :], h_tok[:, t, :])
            ins.then_inc(msq_ready, 1)
            inverse_root(1, RMS_X, NT)

            dve.wait_ge(silu_ready, 1)

            def segment(acc, uses, seg, i=None):
                for j in range(KD):
                    k = 16 * (uses + j // ADA_SLOTS + 1)
                    dve.wait_ge(ada_in[j % ADA_SLOTS], k if i is None else i * (16 * 2 * KD // ADA_SLOTS) + k)
                    w = ada_ring[:, j % ADA_SLOTS, :]
                    if j:
                        dve.wait_ge(ada_used, seg * KD + j if i is None else i * (2 * KD) + (seg * KD + j))
                        ins = v.scalar_tensor_tensor(out=acc, in0=w, scalar=csil[:, j:j + 1], in1=acc,
                                                     op0=ALU.mult, op1=ALU.add)
                    else:
                        ins = v.tensor_scalar(acc, w, csil[:, 0:1], None, ALU.mult)
                    ins.then_inc(ada_used, 1)

            segment(ada_acc[0], 0, 0)
            dve.wait_ge(ada_cols, 1)
            v.tensor_tensor(shift_row.rearrange("p (a b) -> p a b", a=4), shift_row.rearrange("p (a b) -> p a b", a=4),
                            PS[:, 4:8, :], ALU.add).then_inc(ada_taken, 1)
            segment(ada_acc[0], 4, 1)
            dve.wait_ge(ada_cols, 2)
            v.tensor_tensor(scale_row.rearrange("p (a b) -> p a b", a=4), scale_row.rearrange("p (a b) -> p a b", a=4),
                            PS[:, 4:8, :], ALU.add).then_inc(ada_taken, 1)
            dve.wait_ge(ada_taken, 2)
            link(v.scalar_tensor_tensor(out=scale_row, in0=scale_row, scalar=1.0, in1=gain_row, op0=ALU.add, op1=ALU.mult))

            def modulate(dst, src, col, scale, shift, ready):
                for t in range(NT):
                    link(v.scalar_tensor_tensor(out=dst[:, t, :], in0=src[:, t, :], scalar=rstd[:, col + t:col + t + 1],
                                                in1=scale, op0=ALU.mult, op1=ALU.mult))
                    v.tensor_tensor(dst[:, t, :], dst[:, t, :], shift, ALU.add).then_inc(ready, 1)
            modulate(h_tok, X, RMS_X, scale_row, shift_row, htok_ready)

            def bank_out(n, dst):
                dve.wait_ge(tr_done, n + 1)
                v.tensor_copy(dst, PS[:, 4 + n % 4, :].rearrange("p (a b) -> p a b", b=P)).then_inc(tr_out[1], 1)
            for n in range(1, TB_H, 2):
                a, t = h_place(n)
                bank_out(n, hT[:, a:a + 4, t * P:(t + 1) * P])

            dve.wait_ge(htok_ready, NT)
            with dve.Fori(0, 2) as i:
                for k in range(2):
                    dve.wait_ge(ada_cols, i * 2 + (k + 1))
                    segment(ada_acc[1 - k], 4 * (2 + k), 2 + k, i)

            def rotate(parts, tmp, sin, cos):
                for a, b in [parts]:
                    v.tensor_tensor(tmp[0], a, cos, ALU.mult)
                    v.tensor_tensor(tmp[1], b, sin, ALU.mult)
                    v.tensor_tensor(tmp[2], b, cos, ALU.mult)
                    link(v.tensor_tensor(tmp[3], a, sin, ALU.mult))
                    v.tensor_tensor(a, tmp[0], tmp[1], ALU.subtract)
                    return v.tensor_tensor(b, tmp[2], tmp[3], ALU.add)

            dve.wait_ge(sin_ready, 2)
            dve.wait_ge(pj_out, 2 + CH_MAIN + CH_TAIL)
            H8 = NROPE // 2
            for t in range(NT):
                sin, cos = sincos[:, 0, t, 0:16:2], sincos[:, 1, t, 0:16:2]
                q = proj[:, t, Q0:KV0].rearrange("p (h d) -> p h d", d=HD)
                bc = lambda s_: s_.unsqueeze(1).to_broadcast([P, HEADS, H8])
                link(rotate((q[:, :, 0:H8], q[:, :, H8:NROPE]), [ropeT[:, k, t, :, :] for k in range(4)], bc(sin), bc(cos)))
                for b in range(3):
                    k0 = KV0 + b * 2 * GROUPS * HD
                    kk = proj[:, t, k0:k0 + GROUPS * HD].rearrange("p (g d) -> p g d", d=HD)
                    bk = lambda s_: s_.unsqueeze(1).to_broadcast([P, GROUPS, H8])
                    link(rotate((kk[:, :, 0:H8], kk[:, :, H8:NROPE]), [ropeT[:, k, t, 0:GROUPS, :] for k in range(4)],
                                bk(sin), bk(cos)))
            H16 = MROPE // 2
            kr = proj[:, :, KR0:KR0 + MROPE]
            tmp = [ropeT[:, k, :, 0:2, :].rearrange("p t a b -> p t (a b)") for k in range(4)]
            rotate((kr[:, :, 0:H16], kr[:, :, H16:MROPE]), tmp, sincos[:, 0, :, :], sincos[:, 1, :, :]).then_inc(rope_ready, 1)

            junk = at(o_a + 34 * KW, MQ)
            for n, (c0, w) in enumerate(((CQ0, MQ), (CKV0, MKV))):
                for t in range(NT):
                    link(mean_square(RMS_LAT + 2 * n + t, proj[:, t, c0:c0 + w], junk[:, 0:w]))
            dve.sem_inc(msq_ready, 1)
            inverse_root(2, RMS_LAT, 4)
            for n, (c0, w, g_row) in enumerate(((CQ0, MQ, qg_row), (CKV0, MKV, kvg_row))):
                for t in range(NT):
                    lat = proj[:, t, c0:c0 + w]
                    col = RMS_LAT + 2 * n + t
                    ins = v.scalar_tensor_tensor(out=lat, in0=lat, scalar=rstd[:, col:col + 1], in1=g_row[:, :],
                                                 op0=ALU.mult, op1=ALU.mult)
            ins.then_inc(lat_ready, 1)
            bank_out(NB_LAT, cqT[:, :, 0:P])
            dve.wait_ge(tr_done, NB_LAT + 3)
            v.tensor_copy(ckvT.rearrange("p j t -> p (j t)"), PS[:, 4 + (NB_LAT + 2) % 4, :]).then_inc(tr_out[1], 1)

            for b in range(4):
                dve.wait_ge(kt2_in, b + 1)
                ins = v.tensor_copy(KT2[0:HD, b // 2, 2 * (b % 2):2 * (b % 2) + 2, :],
                                    PS[0:HD, b, :].rearrange("p (g t) -> p g t", g=2))
            link(ins)
            dve.wait_ge(kt2_ready, 4)
            dve.wait_ge(tr_out[0], NB_CMP // 2 + 1)
            for s in range(2):
                for hi in range(2):
                    raw = KT2[:, s, :, :].rearrange("p g (b l) -> p l g b", l=CS)[:, 0:CS:2, :, hi:hi + NCMP]
                    pe_c = cmp_cols[:, s * 16 + hi * 8:s * 16 + hi * 8 + 8]
                    pe_c = pe_c.unsqueeze(2).unsqueeze(3).to_broadcast([P, 8, GROUPS, NCMP])
                    ins = v.tensor_tensor(cmpX[:, s, hi * 8:hi * 8 + 8, :].rearrange("p l (g b) -> p l g b", g=GROUPS),
                                          raw, pe_c, ALU.add)
                ins.then_inc(cmpx_ready, 1)
            link(v.memset(cmpHrep, 0.0))
            link(v.memset(Pc, 0.0))
            dve.wait_ge(cmph_ready, 2)
            for h in range(2):
                src = cmpH[:, 1, h, :].rearrange("p (g b) -> p g b", g=GROUPS)
                for copy in range(4):
                    ins = v.tensor_copy(cmpHrep[:, h, :, copy, 0:NCMP], src)
                ins.then_inc(cmprep_ready, 1)
            dve.wait_ge(cmpkv_in, 1)
            v.tensor_copy(kcT.rearrange("p g b -> p (g b)"), PS[:, 0, 0:GROUPS * NCMP]).then_inc(cmpkv_ready, 1)
            dve.wait_ge(cmpkv_in, 2)
            v.tensor_copy(vc.rearrange("p g d -> p (g d)"), PS[:, 2, 0:GROUPS * HD]).then_inc(cmpkv_ready, 1)
            dve.wait_ge(pj_out, 2 + N_KVUP)
            for t in range(NT):
                q = qm[:, t, :].rearrange("p (h d) -> p h d", d=MD)
                bc = lambda s_: s_.unsqueeze(1).to_broadcast([P, HEADS, H16])
                tmp = [at(o_r + (8 + k) * KW, HEADS, H16) for k in range(4)]
                ins = rotate((q[:, :, MN:MN + H16], q[:, :, MN + H16:MD]), tmp, bc(sincos[:, 0, t, :]), bc(sincos[:, 1, t, :]))
                link(ins) if t == 0 else ins.then_inc(qm_roped, 1)

            def mask_max(n, i, step):
                r = n % 2
                dve.wait_ge(s_in, i * step + (n + 1))
                dve.wait_ge(pt_in, i * step + (n + 1))
                dve.sem_inc(dve_passed, 1)
                v.tensor_tensor_reduce(s_prob[:, r, 0:P], PS[:, r, 0:P], causal[:, P:2 * P], 1.0, NEG * 3, ALU.add,
                                       ALU.max, smax[:, r, 0:1])
                v.tensor_tensor_reduce(s_prob[:, r, P:3 * P], PS[:, r, P:3 * P], causal[:, :], 1.0, NEG * 3, ALU.add,
                                       ALU.max, smax[:, r, 1:2]).then_inc(s_free, 1)
                dve.wait_ge(s_free, i * step + (n + 3))

            def minus_max(n, scale):
                v.tensor_scalar(nmax[:, n % 2, :], smax[:, n % 2, :], -scale, None, ALU.mult).then_inc(prob_in, 1)

            def output(n, i, step, place, gate=None):
                dve.wait_ge(prob_ready, i * step + (n + 1))
                link(v.reciprocal(srec[:, n % 2, :], ssum[:, n % 4, :]))
                if gate is not None:
                    link(v.tensor_tensor(srec[:, n % 2, :], srec[:, n % 2, :], gate, ALU.mult))
                dve.wait_ge(o_in, i * step + (n + 3))
                for t in range(NT):
                    src = PS[:, 4 + n % 2, t * HD:(t + 1) * HD]
                    if gate is None:
                        ins = v.tensor_scalar(place(t), src, srec[:, n % 2, t:t + 1], None, ALU.mult)
                    else:
                        ins = v.scalar_tensor_tensor(out=place(t), in0=src, scalar=srec[:, n % 2, t:t + 1], in1=place(t),
                                                     op0=ALU.mult, op1=ALU.add)
                ins.then_inc(o_free, 1)

            U = 2 * RPG
            with dve.Fori(0, GROUPS) as g:
                ch.enter(g, 22)
                dve.wait_ge(heads_in, g * 2 + 2)
                v.tensor_copy(kT.rearrange("p b t -> p (b t)"), PS[:, 7, :]).then_inc(kT_ready, 1)
                dve.wait_ge(csc_in, g * 2 + 2)
                cm = cmask[:, :, :].unsqueeze(2).to_broadcast([P, NT, RPG // 2, NCMP])
                cm01 = cmask01[:, :, :].unsqueeze(2).to_broadcast([P, NT, RPG, NCMP])
                csc4 = csc[:, :, :].rearrange("p (t r) b -> p t r b", t=NT)
                for odd in range(2):
                    cps = PS[:, 7 - odd, 0:P].rearrange("p (t r b) -> p t r b", t=NT, r=RPG)[:, :, odd:RPG:2, 0:NCMP]
                    ins = v.tensor_tensor(csc4[:, :, odd:RPG:2, :], cps, cm, ALU.add)
                link(ins)
                link(v.tensor_reduce(cstat[:, 0, :], csc[:, :, :], AX_X, ALU.max))
                v.tensor_tensor(csc[:, :, :], csc[:, :, :], cstat[:, 0, :].unsqueeze(2).to_broadcast([P, 8, NCMP]),
                                ALU.subtract).then_inc(cexp_in, 1)
                dve.wait_ge(cexp_ready, g + 1)
                link(v.tensor_reduce(cstat[:, 1, :], csc[:, :, :], AX_X, ALU.add))
                link(v.reciprocal(cstat[:, 2, :], cstat[:, 1, :]))
                gate0 = gst[:, :, 0:3 * RPG:3]
                link(v.tensor_tensor(cstat[:, 3, :].rearrange("p (t r) -> p t r", t=NT),
                                     cstat[:, 2, :].rearrange("p (t r) -> p t r", t=NT), gate0, ALU.mult))
                link(v.tensor_tensor(csc[:, :, :], csc[:, :, :], cstat[:, 3, :].unsqueeze(2).to_broadcast([P, 8, NCMP]),
                                     ALU.mult))
                v.tensor_tensor(Pc[:, :, :, 0:NCMP], csc4, cm01, ALU.mult).then_inc(cprob_ready, 1)
                dve.wait_ge(grp_free, g + 1)
                for n in range(U + 2):
                    if n < U:
                        mask_max(n, g, U)
                        minus_max(n, NSA_SCALE)
                    if n == 1:
                        dve.wait_ge(pct_in, g + 1)
                        v.tensor_copy(PcT.rearrange("p t q -> p (t q)"), PS[:, 6, 0:2 * P]).then_inc(pct_ready, 1)
                        dve.wait_ge(oc_in, g + 1)
                        for t in range(NT):
                            ins = v.tensor_copy(ogrp[:, t, 0:RPG, :],
                                                PS[:, 7, t * RPG * HD:(t + 1) * RPG * HD].rearrange("p (r d) -> p r d", d=HD))
                    if n >= 2:
                        r, b = (n - 2) // 2, (n - 2) % 2
                        output(n - 2, g, U, lambda t: ogrp[:, t, r, :], gst[:, :, 3 * r + b + 1])
                dve.wait_ge(o_free, g * U + (U + 2))
                v.memset(smax[:, 0, :], 0.0).then_inc(grp_ready, 1)
                ch.leave(GROUPS)

            M = MLA_BODY
            with dve.Fori(0, HEADS // M) as i:
                ch.enter(i, 8)
                def heads_out(r):
                    dve.wait_ge(mt_in, i * M + (r + 3))
                    v.tensor_copy(mT[0:MD, r % 2, :, :].rearrange("p a b -> p (a b)"), PS[0:MD, 6 + r % 2, :]).then_inc(
                        mt_ready, 1)
                dve.wait_ge(grp_free, i + (GROUPS + 1))
                heads_out(0)
                for n in range(M + 2):
                    if n + 1 < M:
                        if n >= 1:
                            dve.wait_ge(s_in, i * M + (NSA_UNITS + n))
                        heads_out(n + 1)
                    if n < M:
                        mask_max(NSA_UNITS + n, i, M)
                        minus_max(NSA_UNITS + n, MLA_SCALE)
                    if n >= 2:
                        output(NSA_UNITS + n - 2, i, M, lambda t: ogrp[:, t, n - 2, :])
                dve.wait_ge(o_free, i * M + (NSA_UNITS + M + 2))
                v.memset(smax[:, 0, :], 0.0).then_inc(grp_ready, 1)
                ch.leave(HEADS // M)

            for n in range(NB_O + 1, NB_O + TB_O, 2):
                a, t = oT_place(n - NB_O)
                bank_out(n, oT[:, a:a + 4, t * P:(t + 1) * P])

            def mod_row_in(dst, landed, gain, plus_one):
                dve.wait_ge(row_in, landed)
                link(v.tensor_tensor(dst, dst, bias_tmp, ALU.add))
                if gain is not None:
                    link(v.scalar_tensor_tensor(out=dst, in0=dst, scalar=1.0 if plus_one else 0.0, in1=gain,
                                                op0=ALU.add, op1=ALU.mult))
            for dst, landed, gain, one in ((gate_a_row, 48, gain_tmp, False), (shift_f_row, 80, None, False),
                                           (scale_f_row, 128, gain_tmp, True)):
                mod_row_in(dst, landed, gain, one)
                v.memset(smax[:, 0, :], 0.0).then_inc(row_used, 1)

            with dve.Fori(0, 2) as i:
                ch.enter(i, 8)
                for c_ in range(2):
                    dve.wait_ge(w_used, i * 16 + (W_BR + 8 * (c_ + 1)))
                    for t in range(NT):
                        cols = bass.ds(i * (2 * NC) + c_ * NC, NC)
                        for b in range(2):
                            ins = v.tensor_tensor(mtmp[:, t, b, :], PS[:, 4 * c_ + 2 * t + b, :], gates[:, t, b, cols],
                                                  ALU.mult)
                            if t == NT - 1 and b == 1:
                                ins.then_inc(br_out, 1)
                            else:
                                ch.did(ins)
                    dve.wait_ge(br_out, i * 2 + (c_ + 3))
                    ch.wait()
                    for t in range(NT):
                        ins = v.tensor_tensor(merged[:, t, cols], mtmp[:, t, 0, :], mtmp[:, t, 1, :], ALU.add)
                    link(ins)
                ch.leave(2)
            ch.wait()
            v.memset(smax[:, 0, :], 0.0).then_inc(merged_ready, 1)
            for n in range(NB_M + 1, NB_M + TB_M, 2):
                a, t = h_place(n - NB_M)
                bank_out(n, mergedT[:, a:a + 4, t * P:(t + 1) * P])

            dve.wait_ge(pj_out, 2 + N_OUT + 4)
            for t in range(NT):
                ins = mean_square(RMS_Y + t, y[:, t, :], at(o_t + 8 * t * KW, D))
            ins.then_inc(msq_ready, 1)
            for n in range(NB_SK + 1, NB_SK + TB_SK, 2):
                bank_out(n, skT[:, 4 * (n - NB_SK):4 * (n - NB_SK) + 4, :])
            inverse_root(3, RMS_Y, NT)

            def add_branch(t, src, col, row):
                link(v.scalar_tensor_tensor(out=src, in0=src, scalar=rstd[:, col:col + 1], in1=row,
                                            op0=ALU.mult, op1=ALU.mult))
                return v.tensor_tensor(X[:, t, :], X[:, t, :], src, ALU.add)
            for t in range(NT):
                link(add_branch(t, y[:, t, :], RMS_Y + t, gate_a_row))
            for t in range(NT):
                ins = mean_square(RMS_X1 + t, X[:, t, :], at(o_t + 8 * t * KW, D))
            ins.then_inc(msq_ready, 1)
            inverse_root(4, RMS_X1, NT)
            modulate(h2, X, RMS_X1, scale_f_row, shift_f_row, h2_ready)
            for n in range(NB_H2 + 1, NB_H2 + TB_H2, 2):
                a, t = h_place(n - NB_H2)
                bank_out(n, hT[:, a:a + 4, t * P:(t + 1) * P])
            mod_row_in(gate_f_row, 128 + 48, yacc, False)
            v.memset(zeros, 0.0).then_inc(zeros_ready, 1)

            dve.wait_ge(consts, 7)
            link(v.tensor_copy(iota_f[:, :], iota_i[:, :]))

            def settled():
                ch.wait()
                dve.sem_inc(dve_passed, 1)

            def top16(row, values, work):
                ch.did(v.max(top[:, row, 0:8], values))
                settled()
                v.max_index(topi[:, row, 0:8], top[:, row, 0:8], values)
                ch.did(v.match_replace(work, top[:, row, 0:8], values, -3e38))
                settled()
                ch.did(v.max(top[:, row, 8:16], work))
                settled()
                ch.did(v.max_index(topi[:, row, 8:16], top[:, row, 8:16], work))
                settled()

            def topk_parts(u):
                def halves(s):
                    if s == 0:
                        dve.wait_ge(idx_taken, u + 1)
                        dve.wait_ge(sst_ready, u + 1)
                        dve.sem_inc(dve_passed, 1)
                    top16(s, sst[:, s, :], stmp[:, 0:NK])

                def candidates():
                    link(v.tensor_tensor(cand, top[:, 0, :].unsqueeze(2).to_broadcast([P, TOPK, TOPK]),
                                         top[:, 1, :].unsqueeze(1).to_broadcast([P, TOPK, TOPK]), ALU.add))
                    dve.sem_inc(dve_passed, 1)
                    top16(2, cand.rearrange("p a b -> p (a b)"), stmp)
                    v.tensor_scalar(gate_s[:, 0:1], top[:, 2, 0:1], -1.0, None, ALU.mult).then_inc(top_ready, 1)

                def experts():
                    ch.did(v.tensor_scalar(ab_u[:, 0, :], topi[:, 2, :], 4, None, ALU.logical_shift_right))
                    ch.did(v.tensor_scalar(ab_u[:, 1, :], topi[:, 2, :], TOPK - 1, None, ALU.bitwise_and))
                    link(v.tensor_copy(topf[:, :, :], topi[:, 0:2, :]))
                    link(v.tensor_copy(ab_f[:, :, :], ab_u[:, :, :]))
                    link(v.tensor_tensor(onehot, ab_f[:, :, :].unsqueeze(3).to_broadcast([P, 2, TOPK, TOPK]),
                                         iota_f[:, :].unsqueeze(1).unsqueeze(1).to_broadcast([P, 2, TOPK, TOPK]),
                                         ALU.is_equal))
                    link(v.tensor_tensor(onehot, onehot, topf[:, :, :].unsqueeze(2).to_broadcast([P, 2, TOPK, TOPK]),
                                         ALU.mult))
                    link(v.tensor_reduce(i12[:, :, :], onehot, AX_X, ALU.add))
                    v.scalar_tensor_tensor(out=idx_next[:, :], in0=i12[:, 0, :], scalar=float(NK), in1=i12[:, 1, :],
                                           op0=ALU.mult, op1=ALU.add).then_inc(idx_ready, 1)
                    dve.wait_ge(gexp_ready, u + 1)
                    link(v.reciprocal(gate_s[:, 2:3], gate_s[:, 1:2]))
                    link(v.tensor_scalar(gate_next[:, :], gate_e[:, :], gate_s[:, 2:3], None, ALU.mult))

                return [lambda: halves(0), lambda: halves(1), candidates, experts]

            TOPK_STEPS = 22

            def unit(u, t, last=False):
                link(v.tensor_copy(gate_now[:, :], gate_next[:, :]))
                parts = [] if last else topk_parts(u + 1)

                def coefs(b):
                    cols = slice(b * BATCH, (b + 1) * BATCH)
                    dve.wait_ge(gelu_ready, u * 4 + (b + 1))
                    v.tensor_tensor(coef[:, cols], act_g[:, cols], gate_now[:, cols], ALU.mult).then_inc(coef_ready, 1)
                for b in range(TOPK // BATCH):
                    for e in range(b * BATCH, (b + 1) * BATCH):
                        dve.wait_ge(u_in[e % RING], u * 32 + 16 * (e // RING + 1))
                        row = Urow[e % RING]
                        v.tensor_tensor_reduce(row, row, h2[:, t, :], 1.0, 0.0, ALU.mult, ALU.add,
                                               dots[:, e:e + 1]).then_inc(u_free, 1)
                    if parts:
                        parts[b]()
                    coefs(b)
                dve.wait_ge(coef_ready, u * 4 + 4)

            def finish(t):
                dve.wait_ge(y_ready, t + 1)
                v.tensor_tensor_reduce(PS[:, 4 * t:4 * t + 4, :].rearrange("p a b -> p (a b)"), yacc, yacc, 1.0 / D, EPS,
                                       ALU.mult, ALU.add, msq[:, RMS_F + t:RMS_F + t + 1]).then_inc(msq_ready, 1)
                inverse_root(5 + t, RMS_F + t, 1)
                add_branch(t, yacc, RMS_F + t, gate_f_row).then_inc(out_ready, 1)

            for part in topk_parts(0):
                part()
            with dve.Fori(0, PH) as u:
                ch.enter(u, TOPK_STEPS + 1)
                unit(u, 0)
                ch.leave(PH)
            finish(0)
            with dve.Fori(0, PH - 1) as u:
                ch.enter(u, TOPK_STEPS + 1)
                unit(u + PH, 1)
                ch.leave(PH - 1)
            unit(2 * PH - 1, 1, last=True)
            finish(1)


_INS = ["x", "c", "positions", "ada_w", "ada_b", "attn_pre_g", "attn_post_g", "w_in", "cmp_pe", "cmp_w1", "cmp_b1",
        "cmp_w2", "mla_q_norm_g", "mla_w_q_up", "mla_kv_norm_g", "mla_w_kv_up", "w_branch_nsa", "w_branch_mla", "w_out",
        "ffn_pre_g", "ffn_post_g", "peer_w_q", "peer_sub_keys", "peer_u", "peer_v"]


def kernel(**inputs):
    import numpy as _np
    import concourse.bacc as _bacc
    from concourse import mybir as _mybir
    from concourse.bass_utils import run_bass_kernel_spmd as _run

    nc = _bacc.Bacc("TRN2", target_bir_lowering=False, num_devices=1)
    arrays, args = {}, []
    for name in _INS:
        a = _np.ascontiguousarray(inputs[name])
        arrays[f"in_{name}_dram"] = a
        args.append(nc.dram_tensor(f"in_{name}_dram", a.shape, _mybir.dt.from_np(a.dtype), kind="ExternalInput").ap())
    out = nc.dram_tensor("out_0_dram", (1, SEQ, D), _mybir.dt.float32, kind="ExternalOutput").ap()
    build(nc, *args, out)
    r = _run(nc, [arrays], core_ids=[0])
    return r.results[0]["out_0_dram"]
```

```python
from contextlib import ExitStack

import numpy as np
import concourse.bass as bass
from concourse import mybir

ALU = mybir.AluOpType
ACT = mybir.ActivationFunctionType
AX_X = mybir.AxisListType.X
F32 = mybir.dt.float32
F32R = mybir.dt.float32r
I32 = mybir.dt.int32
U32 = mybir.dt.uint32

P = 128
D = 2048
SEQ = 256
NT = SEQ // P
KD = D // P
NC = 512

HEADS, GROUPS, HD = 16, 4, 64
RPG = HEADS // GROUPS
NROPE, MROPE = 16, 32
CB, CS, CH = 32, 16, 256
NCMP = (SEQ - CB) // CS + 1
MQ, MKV, MN = 512, 256, 64
MD = MN + MROPE
Q0 = 0
KV0 = Q0 + HEADS * HD
G0 = KV0 + 3 * 2 * GROUPS * HD
CQ0 = G0 + 3 * HEADS
CKV0 = CQ0 + MQ
KR0 = CKV0 + MKV
GM0 = KR0 + MROPE
EPS = 1e-6
NEG = -1e30
NSA_SCALE = HD ** -0.5
MLA_SCALE = MD ** -0.5

PH, NK, TOPK = 8, 128, 16
RING = 8
BATCH = 4

WSLOTS = 8
ADA_SLOTS = 4
NSEG = 6

TWO_PI = 2.0 * np.pi
PI_PARTS = (6.28125, 0.0019340515136718750, 1.2556659146e-06)
MAGIC = 12582912.0
PI_CLAMP = 3.1415925


class Chain:

    def __init__(self, eng, sem):
        self.eng, self.sem, self.n, self.i, self.step = eng, sem, 0, None, 0

    def did(self, ins):
        ins.then_inc(self.sem, 1)
        self.n += 1
        return ins

    def wait(self):
        self.eng.wait_ge(self.sem, self.n if self.i is None else self.i * self.step + self.n)

    def link(self, ins):
        self.did(ins)
        self.wait()

    def enter(self, i, step):
        self.i, self.step, self.n0 = i, step, self.n

    def leave(self, times):
        assert self.n - self.n0 == self.step, (self.n - self.n0, self.step)
        self.n, self.i = self.n0 + times * self.step, None


def build(nc, x, c, positions, ada_w, ada_b, attn_pre_g, attn_post_g, w_in, cmp_pe, cmp_w1, cmp_b1, cmp_w2,
          mla_q_norm_g, mla_w_q_up, mla_kv_norm_g, mla_w_kv_up, w_branch_nsa, w_branch_mla, w_out,
          ffn_pre_g, ffn_post_g, peer_w_q, peer_sub_keys, peer_u, peer_v, out):
    mod_dram = nc.dram_tensor("mod_rows", [4, D], F32).ap()

    x_v = x.rearrange("o (t p) d -> p (o t) d", p=P)
    out_v = out.rearrange("o (t p) d -> p (o t) d", p=P)
    ada_v = ada_w.rearrange("l (p j) n -> p (l j) n", p=P)
    def rows(w):
        return w.rearrange("l (j p) n -> p (l j) n", p=P)
    win_v, qup_v, kvup_v = rows(w_in), rows(mla_w_q_up), rows(mla_w_kv_up)
    wn_v, wm_v, wo_v, wpq_v = rows(w_branch_nsa), rows(w_branch_mla), rows(w_out), rows(peer_w_q)
    w1_v = cmp_w1.rearrange("l s (j p) n -> p (l s) j n", p=P)
    u_tab = peer_u.rearrange("l e d -> (l e) d")
    v_tab = peer_v.rearrange("l e d -> (l e) d")

    with ExitStack() as ctx:
        def sem(name):
            return ctx.enter_context(nc.semaphore(name))

        KW = 256
        XR, WR, PR, GR, TR, AR, RR = 16, 32, 27, 32, 16, 36, 24
        WORK = 17
        total = XR + WR + PR + GR + TR + AR + RR + WORK
        arena_at = -(-nc.sbuf_base // 32) * 32
        arena = ctx.enter_context(nc.sbuf_tensor("arena", [P, total * KW], F32))
        o_x = 0
        o_w = o_x + XR * KW
        o_p = o_w + WR * KW
        o_g = o_p + PR * KW
        o_t = o_g + GR * KW
        o_a = o_t + TR * KW
        o_r = o_a + AR * KW
        o_k = o_r + RR * KW

        def at(off, *dims):
            n = int(np.prod(dims))
            v = arena[:, off:off + n]
            names = ["a", "b", "c", "d", "e"][:len(dims)]
            if len(dims) > 1:
                v = v.rearrange("p (" + " ".join(names) + ") -> p " + " ".join(names), **dict(zip(names, dims)))
            return v

        def split_at(name, off, *dims, dt=F32R):
            return nc.alloc_sbuf_tensor_at(name, [P, *dims], dt, offset=arena_at + 4 * off)

        X = at(o_x, NT, D)
        wring = at(o_w, WSLOTS, 2, NC)
        w1ring = at(o_w, WSLOTS, 4, CH)
        proj = at(o_p, NT, GM0)
        gates = at(o_g, NT, 2, D)
        h_tok = at(o_g, NT, D)
        hT = at(o_t, KD, SEQ)
        ada_acc = [at(o_k, D), at(o_r, D)]
        ada_ring = at(o_a, ADA_SLOTS, D)
        shift_row = at(o_r, D)
        scale_row = at(o_r + 8 * KW, D)
        gain_row = at(o_r + 16 * KW, D)
        mod_row = at(o_r + 16 * KW, D)
        KT2 = at(o_t, 2, GROUPS, SEQ)
        cmpX = at(o_t + 8 * KW, 2, CB // 2, GROUPS * NCMP)
        qm = at(o_a, NT, HEADS * MD)
        kvm = at(o_a + 12 * KW, NT, HEADS * 2 * MN)
        cqT = at(o_a + 28 * KW, 4, SEQ)
        ckvT = at(o_a + 32 * KW, 2, SEQ)
        kdup = at(o_r, 2, NT, GROUPS, 2, HD)
        cmpHrep = at(o_r + 8 * KW, 2, GROUPS, 4, 32)
        cmpH = at(o_r + 12 * KW, 2, 2, GROUPS * NCMP)
        Pc = at(o_r + 13 * KW, NT, RPG, 32)
        PcT = at(o_r + 14 * KW, NT, P)
        ogrp = at(o_r + 15 * KW, NT, 8, HD)
        s_prob = at(o_r + 19 * KW, 2, 384)
        vcg = at(o_r + 22 * KW, RPG, HD)
        o_nsa = at(o_t, NT, HEADS * HD)
        o_mla = at(o_t + 8 * KW, NT, HEADS * HD)
        qst = at(o_k, NT, RPG * HD)
        kst = at(o_k + 2 * KW, 2, NT, 2, HD)
        qT = at(o_k + 4 * KW, 2, NT, P)
        kT = at(o_k + 6 * KW, 2, SEQ)
        mst = at(o_k, 2, 2, NT, MD)
        mT = at(o_k + 3 * KW, 2, 4, P)
        probT = at(o_k + 8 * KW, 2, 384)
        ropeT = at(o_r + 8 * KW, 4, NT, HEADS, 8)
        qg_row = at(o_k + 11 * KW, MQ)
        kvg_row = at(o_k + 13 * KW, MKV)
        w2k = at(o_k + 14 * KW, 2, 2, HD)
        w2v = at(o_k + 15 * KW, 2, HD)
        vc = at(o_k + 15 * KW + KW // 2, GROUPS, HD)
        y = at(o_a + 16 * KW, NT, D)
        bias_tmp = at(o_k + 8 * KW, D)
        gain_tmp = at(o_p + 16 * KW, D)
        merged = at(o_p, NT, D)
        gate_a_row = at(o_r, D)
        shift_f_row = at(o_r + 8 * KW, D)
        scale_f_row = at(o_r + 16 * KW, D)
        mtmp = at(o_k, 2, 2, NC)
        SPLIT = 4
        w_raw = split_at("w_raw", o_w, SPLIT, 2, NC, dt=F32)
        w_lo = split_at("w_lo", o_w, SPLIT, 2, NC)
        w_hi = split_at("w_hi", o_w + 16 * KW, SPLIT, 2, NC)
        oT_hi, oT_lo = split_at("oT_hi", o_a, 16, SEQ), split_at("oT_lo", o_a + 16 * KW, 16, SEQ)
        mergedT_hi, mergedT_lo = split_at("mergedT_hi", o_t, KD, SEQ), split_at("mergedT_lo", o_a, KD, SEQ)
        h2T_hi, h2T_lo = split_at("h2T_hi", o_t, KD, SEQ), split_at("h2T_lo", o_a, KD, SEQ)
        h2 = at(o_g, NT, D)
        qryT = at(o_g + 16 * KW, 2 * PH, SEQ)
        sk_raw = at(o_p, 2 * PH, P)
        skT = at(o_p + 8 * KW, 2 * PH, NK)
        scores = at(o_a, NT, PH, 2 * NK)
        yacc = at(o_a + 16 * KW, D)
        gate_f_row = at(o_a + 24 * KW, D)
        sst = at(o_a + 32 * KW, 2, NK)
        stmp = at(o_a + 33 * KW, 2 * NK)
        cand = at(o_a + 32 * KW, TOPK, TOPK)
        onehot = at(o_a + 34 * KW, 2, TOPK, TOPK)
        diag = [at(o, P) for o in [o_p + 24 * KW + P * i for i in range(6)] + [o_k + 16 * KW + P * i for i in range(2)]]
        slot_off = ([o_w + 8 * KW * i for i in range(4)] + [o_p + 8 * KW * i for i in range(3)]
                    + [o_g + (16 + 8 * i) * KW for i in range(2)] + [o_t + 8 * KW * i for i in range(2)]
                    + [o_r + 8 * KW * i for i in range(3)] + [o_k + 8 * KW * i for i in range(2)])
        Urow = [at(o, D) for o in slot_off[:RING]]
        Vrow = [at(o, D) for o in slot_off[RING:2 * RING]]

        def sb(name, shape, dt=F32):
            return ctx.enter_context(nc.sbuf_tensor(name, shape, dt))

        ident = sb("ident", [P, P])
        ones = sb("ones", [P, P])
        zeros = ones[:, :]
        causal = sb("causal", [P, 2 * P])
        blocks = sb("blocks", [P, RPG])
        cmask = sb("cmask", [P, NT, NCMP])
        cmask01 = sb("cmask01", [P, NT, NCMP])
        sincos = sb("sincos", [P, 2, NT, 16])
        ang = sb("ang", [P, 3, NT * 16])
        freq = sb("freq", [P, 16])
        pos_i = sb("pos_i", [P, NT], I32)
        pos_f = sb("pos_f", [P, NT])
        ccol = sb("ccol", [P, KD])
        csil = sb("csil", [P, KD])
        msq = sb("msq", [P, 16])
        rstd = sb("rstd", [P, 16])
        cmp_rows = sb("cmp_rows", [36, P])
        cmp_cols = sb("cmp_cols", [P, 36])
        kcT = sb("kcT", [P, GROUPS, NCMP])
        kcg = sb("kcg", [P, NCMP])
        gnsa = sb("gnsa", [P, NT, 3 * HEADS])
        gst = sb("gst", [P, NT, RPG * 3])
        csc = sb("csc", [P, 8, NCMP])
        cstat = sb("cstat", [P, 4, 8])
        smax = sb("smax", [P, 2, NT])
        nmax = sb("nmax", [P, 2, NT])
        ssum = sb("ssum", [P, 4, NT])
        srec = sb("srec", [P, 2, NT])
        eps = sb("eps", [P, 1])
        ysq = sb("ysq", [P, NT, D // NC])
        top = sb("top", [P, 3, TOPK])
        topi = sb("topi", [P, 3, TOPK], U32)
        topf = sb("topf", [P, 2, TOPK])
        ab_u = sb("ab_u", [P, 2, TOPK], U32)
        ab_f = sb("ab_f", [P, 2, TOPK])
        i12 = sb("i12", [P, 2, TOPK])
        iota_i = sb("iota_i", [P, TOPK], I32)
        iota_f = sb("iota_f", [P, TOPK])
        idx_next = sb("idx_next", [P, TOPK], U32)
        idx_now = sb("idx_now", [P, 2, TOPK], U32)
        gate_e = sb("gate_e", [P, TOPK])
        gate_s = sb("gate_s", [P, 4])
        gate_next = sb("gate_next", [P, TOPK])
        gate_now = sb("gate_now", [P, TOPK])
        dots = sb("dots", [P, TOPK])
        act_g = sb("act_g", [P, TOPK])
        coef = sb("coef", [P, TOPK])

        PS = ctx.enter_context(nc.psum_tensor("PS", [P, 8, 512], F32))

        dve_done, act_done, pool_done = sem("dve_done"), sem("act_done"), sem("pool_done")
        dve_passed, pool_passed = sem("dve_passed"), sem("pool_passed")
        x_in, small_in, consts = sem("x_in"), sem("small_in"), sem("consts")
        ada_in = [sem(f"ada_in{i}") for i in range(ADA_SLOTS)]
        ada_used, ada_cols = sem("ada_used"), sem("ada_cols")
        c_in, first_rows_in = sem("c_in"), sem("first_rows_in")
        mod_ready, mod_stored = sem("mod_ready"), sem("mod_stored")
        w_landed = [sem(f"w_landed{i}") for i in range(WSLOTS)]
        w_used = sem("w_used")
        split_in = [sem(f"split_in{i}") for i in range(SPLIT)]
        hi_ready, lo_ready, bank_hi = sem("hi_ready"), sem("lo_ready"), sem("bank_hi")
        msq_ready, root_ready = sem("msq_ready"), sem("root_ready")
        angle_ready, sin_ready, silu_ready = sem("angle_ready"), sem("sin_ready"), sem("silu_ready")
        htok_ready = sem("htok_ready")
        tr_done = sem("tr_done")
        tr_out = [sem("tr_out_act"), sem("tr_out_dve")]
        pj_out = sem("pj_out")
        gnsa_ready = sem("gnsa_ready")
        rope_ready, kdup_ready, kt2_in, kt2_ready, cmpx_ready = (sem("rope_ready"), sem("kdup_ready"), sem("kt2_in"),
                                                                 sem("kt2_ready"), sem("cmpx_ready"))
        cmph_ready, cmprep_ready, cmpkv_in, cmpkv_ready = (
            sem("cmph_ready"), sem("cmprep_ready"), sem("cmpkv_in"), sem("cmpkv_ready"))
        lat_ready, qm_roped = sem("lat_ready"), sem("qm_roped")
        staged, gates_staged, cvalues_staged = sem("staged"), sem("gates_staged"), sem("cvalues_staged")
        heads_in, qT_ready, kT_ready = sem("heads_in"), sem("qT_ready"), sem("kT_ready")
        csc_in, cexp_in, cexp_ready, cprob_ready, pct_in, pct_ready, oc_in = (
            sem("csc_in"), sem("cexp_in"), sem("cexp_ready"), sem("cprob_ready"), sem("pct_in"), sem("pct_ready"),
            sem("oc_in"))
        s_in, s_free, prob_in, prob_ready, pt_in, pt_ready, o_in, o_free = (
            sem("s_in"), sem("s_free"), sem("prob_in"), sem("prob_ready"), sem("pt_in"), sem("pt_ready"),
            sem("o_in"), sem("o_free"))
        grp_ready, grp_free = sem("grp_ready"), sem("grp_free")
        m_staged, mt_in, mt_ready = sem("m_staged"), sem("mt_in"), sem("mt_ready")
        row_in, last_row_in, row_step, rows_ready = sem("row_in"), sem("last_row_in"), sem("row_step"), sem("rows_ready")
        br_out, merged_ready = sem("br_out"), sem("merged_ready")
        h2_ready, sk_in = sem("h2_ready"), sem("sk_in")
        q_out, sc_in, sc_out = sem("q_out"), sem("sc_in"), sem("sc_out")
        sst_ready, top_ready, gexp_ready, idx_ready, idx_taken = (sem("sst_ready"), sem("top_ready"), sem("gexp_ready"),
                                                                  sem("idx_ready"), sem("idx_taken"))
        u_in = [sem(f"u_in{i}") for i in range(RING)]
        v_in = [sem(f"v_in{i}") for i in range(RING)]
        u_free, v_free = sem("u_free"), sem("v_free")
        gelu_ready, coef_ready, diag_ready, y_ready = sem("gelu_ready"), sem("coef_ready"), sem("diag_ready"), sem("y_ready")
        eps_ready, x1_ready = sem("eps_ready"), sem("x1_ready")
        zeros_ready = sem("zeros_ready")
        out_ready, out_stored = sem("out_ready"), sem("out_stored")

        CH_MAIN, CH_TAIL, CH_GATE = 6, 1, 8
        CH_FIRST, QTRS = 2, D // NC
        CH_QUP, CH_KVUP = HEADS * MD // NC, HEADS * 2 * MN // NC
        TAIL = GM0 - CH_MAIN * NC
        N_QUP = CH_MAIN + CH_TAIL + CH_GATE
        N_KVUP = N_QUP + CH_QUP
        N_OUT = N_KVUP + CH_KVUP
        W_TAIL = CH_MAIN * 8
        W_GATE = W_TAIL + 8
        W_CMP = W_GATE + CH_GATE * 8
        W_QUP = W_CMP + 8
        W_KVUP = W_QUP + CH_QUP * 2
        W_BR = W_KVUP + CH_KVUP
        AHEAD = 3
        W_OUT = W_BR + 4 * 8
        W_PQ = W_OUT + 4 * 8
        TB_H, TB_CMP, TB_LAT, TB_O, TB_M, TB_SK, TB_H2 = 8, 1, 3, 8, 8, 4, 8
        NB_CMP = TB_H
        NB_LAT = NB_CMP + TB_CMP
        NB_O = NB_LAT + TB_LAT
        NB_M = NB_O + TB_O
        NB_SK = NB_M + TB_M
        NB_H2 = NB_SK + TB_SK
        NSA_UNITS = GROUPS * RPG * 2
        MLA_BODY = 8
        RMS_X, RMS_LAT, RMS_Y, RMS_X1, RMS_F = 0, 2, 6, 8, 10

        def first_bank(q):
            return 4 + (2 * q + 2) % 4

        def first_acc(seg, odd):
            return ada_acc[0][:, (2 * seg + odd) * NC:(2 * seg + odd + 1) * NC]

        def banks_out(eng, n):
            eng.wait_ge(tr_out[0], (n + 1) // 2)
            if n // 2:
                eng.wait_ge(tr_out[1], n // 2)

        def oT_place(n):
            return 4 * (n // 2), n % 2

        def h_place(n):
            return 4 * (n % 4), n // 4

        block = ctx.enter_context(nc.Block())

        @block.sync
        def _(sp):
            for t in range(NT):
                sp.dma_start(X[:, t, :], x_v[:, t, :]).then_inc(x_in, 16)

            def load(m, src, cols=NC, first=False, i=None, step=0):
                if not first:
                    need = m - WSLOTS + 1
                    sp.wait_ge(w_used, need if i is None else i * step + need)
                sp.dma_start(wring[:, m % WSLOTS, :, 0:cols], src).then_inc(w_landed[m % WSLOTS], 16)

            for m in range(CH_FIRST * 8):
                q, c_, w = m // 4, m // 2 % 2, m % 2
                if m % 4 == 0 and q < 2:
                    sp.wait_ge(ada_used, 2 + 7 * q)
                load(m, win_v[:, 4 * q + 2 * w:4 * q + 2 * w + 2, c_ * NC:(c_ + 1) * NC], first=m < WSLOTS)
            with sp.Fori(0, CH_MAIN - CH_FIRST) as i:
                for k in range(8):
                    load(CH_FIRST * 8 + k, win_v[:, 2 * k:2 * k + 2, bass.ds(i * NC + CH_FIRST * NC, NC)], i=i, step=8)
            for k in range(8):
                load(W_TAIL + k, win_v[:, 2 * k:2 * k + 2, CH_MAIN * NC:GM0], cols=TAIL)
            with sp.Fori(0, CH_GATE) as i:
                for k in range(8):
                    load(W_GATE + k, win_v[:, 2 * k:2 * k + 2, bass.ds(i * NC + GM0, NC)], i=i, step=8)
            for k in range(8):
                sp.wait_ge(w_used, W_CMP + k - WSLOTS + 1)
                sp.dma_start(w1ring[:, (W_CMP + k) % WSLOTS, :, :],
                             w1_v[:, k // 4, 4 * (k % 4):4 * (k % 4) + 4, :]).then_inc(w_landed[(W_CMP + k) % WSLOTS], 16)
            for n in range(CH_QUP):
                for k in range(2):
                    load(W_QUP + 2 * n + k, qup_v[:, 2 * k:2 * k + 2, n * NC:(n + 1) * NC])
            for n in range(CH_KVUP):
                load(W_KVUP + n, kvup_v[:, 0:2, n * NC:(n + 1) * NC])
            def load_split(m, src, i):
                sp.wait_ge(w_used, i * 8 + (m - SPLIT + 1))
                sp.dma_start(w_raw[:, m % SPLIT, :, :], src).then_inc(split_in[m % SPLIT], 16)
            sp.wait_ge(w_used, W_BR)
            with sp.Fori(0, 4) as i:
                for k in range(8):
                    w_v = wn_v if k < 4 else wm_v
                    kk = 2 * (k % 4)
                    load_split(W_BR + k, w_v[:, kk:kk + 2, bass.ds(i * NC, NC)], i)
            for w0, w_v in ((W_OUT, wo_v), (W_PQ, wpq_v)):
                with sp.Fori(0, 4) as i:
                    for k in range(8):
                        load_split(w0 + k, w_v[:, 2 * k:2 * k + 2, bass.ds(i * NC, NC)], i)
                if w0 == W_OUT:
                    banks_out(sp, NB_M + TB_M)
                    sk_v = peer_sub_keys.rearrange("l h s n d -> (l h s) n d")
                    for k in range(2 * PH):
                        sp.dma_start(sk_raw[:, k, :], sk_v[k]).then_inc(sk_in, 16)
            sp.wait_ge(h2_ready, NT)
            sp.dma_start(gate_f_row, mod_dram[3, :].partition_broadcast(P)).then_inc(last_row_in, 16)
            sp.dma_start(bias_tmp, ada_b[0, 5 * D:6 * D].partition_broadcast(P)).then_inc(last_row_in, 16)
            sp.dma_start(yacc, ffn_post_g[0, :].partition_broadcast(P)).then_inc(last_row_in, 16)
            for t in range(NT):
                sp.wait_ge(out_ready, t + 1)
                sp.dma_start(out_v[:, t, :], X[:, t, :]).then_inc(out_stored, 16)
            sp.wait_ge(out_stored, 16 * NT)

        @block.gpsimd
        def _(pool):
            ch = Chain(pool, pool_done)
            def ada_first(n):
                q, seg, j = n // 8, n // 4 % 2, n % 4
                if n >= ADA_SLOTS:
                    pool.wait_ge(ada_used, n - ADA_SLOTS + 1)
                pool.dma_start(ada_ring[:, n % ADA_SLOTS, :].rearrange("p (j n) -> p j n", j=4),
                               ada_v[:, 4 * j:4 * j + 4, seg * D + q * NC:seg * D + (q + 1) * NC]).then_inc(
                    ada_in[n % ADA_SLOTS], 16)

            def ada(j, i):
                n = 2 * KD + j
                pool.wait_ge(ada_used, i * KD + (n - ADA_SLOTS + 1))
                pool.dma_start(ada_ring[:, j % ADA_SLOTS, :], ada_v[:, j, bass.ds(i * D + 2 * D, D)]).then_inc(
                    ada_in[j % ADA_SLOTS], 16)
            for n in range(ADA_SLOTS):
                ada_first(n)
            pool.memset(ident[:, :], 0.0).then_inc(pool_done, 1)
            pool.memset(ones[:, :], 1.0).then_inc(pool_done, 1)
            pool.memset(causal[:, :], 0.0).then_inc(pool_done, 1)
            pool.memset(cmask[:, :, :], 0.0).then_inc(pool_done, 1)
            pool.memset(cmask01[:, :, :], 1.0).then_inc(pool_done, 1)
            ch.n = 5
            ch.wait()
            pool.affine_select(out=ident[:, :], in_=ident[:, :], compare_op=ALU.not_equal, fill=1.0, base=0,
                               pattern=[[-1, P]], channel_multiplier=1).then_inc(consts, 1)
            pool.affine_select(out=causal[:, P:2 * P], in_=causal[:, P:2 * P], compare_op=ALU.is_ge, fill=NEG, base=0,
                               pattern=[[-1, P]], channel_multiplier=1).then_inc(consts, 1)
            for t in range(NT):
                pool.affine_select(out=cmask[:, t, :], in_=cmask[:, t, :], compare_op=ALU.is_ge, fill=NEG,
                                   base=t * P - CB + 1, pattern=[[-CS, NCMP]], channel_multiplier=1).then_inc(consts, 1)
                pool.affine_select(out=cmask01[:, t, :], in_=cmask01[:, t, :], compare_op=ALU.is_ge, fill=0.0,
                                   base=t * P - CB + 1, pattern=[[-CS, NCMP]], channel_multiplier=1).then_inc(consts, 1)
            pool.memset(blocks[:, :], 1.0).then_inc(pool_done, 1)
            pool.wait_ge(pool_done, 6)
            pool.affine_select(out=blocks[:, :], in_=blocks[:, :], compare_op=ALU.is_ge, fill=0.0, base=0,
                               pattern=[[-32, RPG]], channel_multiplier=1).then_inc(pool_done, 1)
            pool.wait_ge(pool_done, 7)
            pool.affine_select(out=blocks[:, :], in_=blocks[:, :], compare_op=ALU.is_ge, fill=0.0, base=31,
                               pattern=[[32, RPG]], channel_multiplier=-1).then_inc(pool_done, 1)
            pool.iota(iota_i[:, :], pattern=[[1, TOPK]], base=0, channel_multiplier=0).then_inc(consts, 1)
            for n in range(ADA_SLOTS, 2 * KD):
                ada_first(n)
            with pool.Fori(0, NSEG - 2) as i:
                for j in range(KD):
                    ada(j, i)

            pool.wait_ge(rope_ready, 1)
            pool.wait_ge(ada_cols, 2 * QTRS + NSEG - 2)
            pool.wait_ge(pj_out, 2 + CH_MAIN)
            for s in range(2):
                for t in range(NT):
                    src = proj[:, t, KV0 + s * GROUPS * HD:KV0 + (s + 1) * GROUPS * HD]
                    src = src.rearrange("p (g d) -> p g d", g=GROUPS)
                    for copy in range(2):
                        pool.tensor_copy(kdup[:, s, t, :, copy, :], src).then_inc(kdup_ready, 1)

            pool.wait_ge(gnsa_ready, 1)
            pool.wait_ge(cmpkv_ready, 2)
            pool.wait_ge(mod_stored, 16 * 5)
            def stage_heads(q0, k0):
                pool.tensor_copy(qst, proj[:, :, bass.ds(q0 + Q0, RPG * HD)]).then_inc(staged, 1)
                for b in range(2):
                    src = proj[:, :, bass.ds(k0 + (KV0 + (b + 1) * 2 * GROUPS * HD), HD)]
                    for copy in range(2):
                        pool.tensor_copy(kst[:, b, :, copy, :], src).then_inc(staged, 1)

            def stage_ckeys(g):
                pool.tensor_copy(kcg[:, :], kcT[:, bass.ds(g, 1), :].rearrange("p a b -> p (a b)")).then_inc(staged, 1)

            def stage_cvalues(g):
                pool.tensor_tensor(vcg, vc[:, bass.ds(g, 1), :].to_broadcast([P, RPG, HD]),
                                   blocks[:, :].unsqueeze(2).to_broadcast([P, RPG, HD]), ALU.mult).then_inc(cvalues_staged, 1)

            def stage_gates(g0):
                pool.tensor_copy(gst[:, :, :], gnsa[:, :, bass.ds(g0, RPG * 3)]).then_inc(gates_staged, 1)

            def group_out(g0):
                pool.tensor_copy(o_nsa[:, :, bass.ds(g0, RPG * HD)].rearrange("p t (r d) -> p t r d", d=HD),
                                 ogrp[:, :, 0:RPG, :]).then_inc(grp_free, 1)
            stage_heads(0, 0)
            stage_ckeys(0)
            stage_gates(0)
            stage_cvalues(0)
            with pool.Fori(0, GROUPS - 1) as g:
                pool.wait_ge(heads_in, g * 2 + 2)
                stage_heads(g * (RPG * HD) + RPG * HD, g * HD + HD)
                pool.wait_ge(csc_in, g * 2 + 2)
                stage_ckeys(g + 1)
                pool.wait_ge(oc_in, g + 1)
                stage_cvalues(g + 1)
                pool.wait_ge(grp_ready, g + 1)
                stage_gates(g * (RPG * 3) + RPG * 3)
                group_out(g * (RPG * HD))
            pool.wait_ge(grp_ready, GROUPS)
            group_out((GROUPS - 1) * RPG * HD)

            pool.wait_ge(qm_roped, 1)
            pool.wait_ge(s_in, NSA_UNITS)
            with pool.Fori(0, HEADS // MLA_BODY) as i:
                for r in range(MLA_BODY):
                    pool.wait_ge(mt_in, i * MLA_BODY + (r + 1))
                    qsrc = qm[:, :, bass.ds(i * (MLA_BODY * MD) + r * MD, MD)]
                    ksrc = kvm[:, :, bass.ds(i * (MLA_BODY * 2 * MN) + r * 2 * MN, MN)]
                    pool.tensor_copy(mst[:, r % 2, 0, :, :], qsrc).then_inc(m_staged, 1)
                    pool.tensor_copy(mst[:, r % 2, 1, :, 0:MN], ksrc).then_inc(m_staged, 1)
                    pool.tensor_copy(mst[:, r % 2, 1, :, MN:MD], proj[:, :, KR0:KR0 + MROPE]).then_inc(m_staged, 1)
                pool.wait_ge(grp_ready, i + (GROUPS + 1))
                pool.tensor_copy(o_mla[:, :, bass.ds(i * (MLA_BODY * HD), MLA_BODY * HD)].rearrange(
                    "p t (r d) -> p t r d", d=HD), ogrp[:, :, :, :]).then_inc(grp_free, 1)

            pool.wait_ge(mod_stored, 16 * 5)
            pool.wait_ge(o_free, 2 + NSA_UNITS + HEADS)
            pool.wait_ge(grp_free, 1 + GROUPS + HEADS // MLA_BODY)
            landed = 0
            for dst, row, seg, gain in ((gate_a_row, 0, 2, attn_post_g), (shift_f_row, 1, 3, None),
                                        (scale_f_row, 2, 4, ffn_pre_g)):
                pool.dma_start(dst, mod_dram[row, :].partition_broadcast(P)).then_inc(row_in, 16)
                pool.dma_start(bias_tmp, ada_b[0, seg * D:(seg + 1) * D].partition_broadcast(P)).then_inc(row_in, 16)
                if gain is not None:
                    pool.dma_start(gain_tmp, gain[0, :].partition_broadcast(P)).then_inc(row_in, 16)
                landed += 32 if gain is None else 48
                pool.wait_ge(row_in, landed)
                pool.tensor_tensor(dst, dst, bias_tmp, ALU.add).then_inc(row_step, 1)
                pool.wait_ge(row_step, 2 * row + 1)
                if row == 2:
                    pool.tensor_scalar(dst, dst, 1.0, None, ALU.add).then_inc(row_step, 1)
                    pool.wait_ge(row_step, 2 * row + 2)
                if gain is not None:
                    pool.tensor_tensor(dst, dst, gain_tmp, ALU.mult).then_inc(rows_ready, 1)
                    pool.wait_ge(rows_ready, 1 + row // 2)
                    if row == 0:
                        pool.sem_inc(row_step, 1)
                else:
                    pool.sem_inc(row_step, 1)

            def unit(u, now):
                pool.wait_ge(idx_ready, u + 1)
                pool.sem_inc(pool_passed, 1)
                pool.tensor_copy(idx_now[:, now, :], idx_next[:, :]).then_inc(idx_taken, 1)
                pool.wait_ge(idx_taken, u + 2)
                pool.sem_inc(pool_passed, 1)
                for b in range(TOPK // BATCH):
                    for tab, ring, free, landed in ((u_tab, Urow, u_free, u_in), (v_tab, Vrow, v_free, v_in)):
                        pool.wait_ge(free, u * TOPK + (b + 1) * BATCH)
                        pool.sem_inc(pool_passed, 1)
                        for e in range(b * BATCH, (b + 1) * BATCH):
                            pool.indirect_dma_start(
                                ring[e % RING], None, tab,
                                bass.IndirectOffsetOnAxis(ap=idx_now[:, now, e:e + 1], axis=0)).then_inc(landed[e % RING], 16)
            pool.wait_ge(sc_out, 8)
            pool.wait_ge(h2_ready, NT)
            with pool.Fori(0, PH) as i:
                for k in range(2):
                    unit(i * 2 + k, k)

        @block.scalar
        def _(act):
            with nc.allow_non_contiguous_dma("a few hundred words"):
                act.dma_start(ccol[:, :], c.rearrange("o (p j) -> (o p) j", p=P)).then_inc(c_in, 16)
            act.dma_start(shift_row, ada_b[0, 0:D].partition_broadcast(P)).then_inc(first_rows_in, 16)
            act.dma_start(scale_row, ada_b[0, D:2 * D].partition_broadcast(P)).then_inc(first_rows_in, 16)
            act.dma_start(gain_row, attn_pre_g[0, :].partition_broadcast(P)).then_inc(first_rows_in, 16)
            with nc.allow_non_contiguous_dma("a few hundred words"):
                act.dma_start(pos_i[:, :], positions.rearrange("o (t p) -> p (o t)", p=P)).then_inc(small_in, 16)
            act.dma_start(qg_row[:, :], mla_q_norm_g[0, :].partition_broadcast(P)).then_inc(small_in, 16)
            act.dma_start(kvg_row[:, :], mla_kv_norm_g[0, :].partition_broadcast(P)).then_inc(small_in, 16)
            act.dma_start(cmp_rows[0:32, :], cmp_pe.rearrange("l s (i e) d -> (l s i) (e d)", e=2)).then_inc(small_in, 16)
            act.dma_start(cmp_rows[32:36, :], cmp_b1.rearrange("l s (h n) -> (l s h) n", n=P)).then_inc(small_in, 16)
            w2_v = cmp_w2.rearrange("l s (h p) d -> p (l s) h d", p=P)
            for copy in range(2):
                act.dma_start(w2k[:, :, copy, :], w2_v[:, 0, :, :]).then_inc(small_in, 16)
            act.dma_start(w2v[:, :, :], w2_v[:, 1, :, :]).then_inc(small_in, 16)
            act.wait_ge(c_in, 16)
            nc.scalar.activation(csil[:, :], ccol[:, :], ACT.Silu).then_inc(silu_ready, 1)

            def root(n, col, cnt):
                act.wait_ge(msq_ready, n)
                nc.scalar.activation(rstd[:, col:col + cnt], msq[:, col:col + cnt], ACT.Sqrt).then_inc(root_ready, 1)

            def bank_out(n, dst, upto=4 * P):
                act.wait_ge(tr_done, n + 1)
                src = PS[:, 4 + n % 4, 0:upto]
                if len(dst.shape) == 3:
                    src = src.rearrange("p (a b) -> p a b", b=P)
                nc.scalar.copy(dst, src).then_inc(tr_out[0], 1)

            root(1, RMS_X, NT)
            for n in range(0, TB_H, 2):
                bank_out(n, hT[:, 2 * n:2 * n + 4, 0:P])

            def chunk_out(n, m_end, dst, func=ACT.Copy, i=None, step=0, tiles=0):
                act.wait_ge(w_used, m_end if i is None else i * (step * tiles) + m_end)
                for t in range(NT):
                    d = dst(t)
                    ins = nc.scalar.activation(d, PS[:, (n % 2) * 2 + t, 0:d.shape[-1]], func)
                ins.then_inc(pj_out, 1)

            def mod_out(r, i):
                act.wait_ge(ada_cols, i * 2 + (2 * QTRS + r + 1))
                act.wait_ge(mod_stored, i * 32 + 16 * (r + 1))
                nc.scalar.copy(mod_row[0:1, :].rearrange("p (a b) -> p a b", a=4), PS[0:1, 4:8, :]).then_inc(mod_ready, 1)
                act.wait_ge(mod_ready, i * 2 + (r + 2))
                act.dma_start(mod_dram[bass.ds(i * 2 + r, 1), :], mod_row[0:1, :]).then_inc(mod_stored, 16)

            for k in range(CH_FIRST):
                chunk_out(k, CH_FIRST * 8 - 2 * (1 - k), lambda t: proj[:, t, k * NC:(k + 1) * NC])
            act.wait_ge(small_in, 16 * 8)
            act.wait_ge(angle_ready, 1)
            nc.scalar.activation(sincos[:, 0, :, :], ang[:, 0, :], ACT.Sin).then_inc(sin_ready, 1)
            nc.scalar.activation(sincos[:, 1, :, :], ang[:, 1, :], ACT.Sin).then_inc(sin_ready, 1)
            with act.Fori(0, (CH_MAIN - CH_FIRST) // 2) as i:
                for k in range(2):
                    chunk_out(k, 8 * (CH_FIRST + k + 1),
                              lambda t: proj[:, t, bass.ds(i * (2 * NC) + (CH_FIRST + k) * NC, NC)], ACT.Copy, i, 2, 8)
            chunk_out(CH_MAIN, W_GATE, lambda t: proj[:, t, CH_MAIN * NC:GM0])
            gates_v = gates.rearrange("p t s d -> p t (s d)")
            with act.Fori(0, 2) as i:
                for k in range(4):
                    chunk_out(CH_MAIN + 1 + k, W_GATE + 8 * (k + 1),
                              lambda t: gates_v[:, t, bass.ds(i * (4 * NC) + k * NC, NC)], ACT.Sigmoid, i, 4, 8)
                    if k % 2:
                        mod_out(k // 2, i)
            act.wait_ge(pj_out, 2 + CH_MAIN)
            nc.scalar.activation(gnsa[:, :, :], proj[:, :, G0:CQ0], ACT.Sigmoid).then_inc(gnsa_ready, 1)

            act.wait_ge(tr_done, NB_CMP + 1)
            nc.scalar.copy(cmp_cols[:, :], PS[:, 4 + NB_CMP % 4, 0:36]).then_inc(tr_out[0], 1)
            root(2, RMS_LAT, 4)
            bank_out(NB_LAT + 1, cqT[:, :, P:2 * P])
            for b in range(4):
                act.wait_ge(kt2_in, b + 1)
                nc.scalar.copy(KT2[HD:P, b // 2, 2 * (b % 2):2 * (b % 2) + 2, 0:SEQ - 1],
                               PS[HD:P, b, :].rearrange("p (g t) -> p g t", g=2)[:, :, 1:SEQ]).then_inc(kt2_ready, 1)
            act.wait_ge(tr_out[0], NB_CMP // 2 + 1)
            for s in range(2):
                act.wait_ge(w_used, W_CMP + 4 * (s + 1))
                for h in range(2):
                    ins = nc.scalar.activation(cmpH[:, s, h, :], PS[:, 2 * s + h, 0:GROUPS * NCMP], ACT.Gelu_apprx_tanh,
                                               bias=cmp_cols[:, 32 + 2 * s + h:33 + 2 * s + h])
                ins.then_inc(cmph_ready, 1)
            for k in range(CH_QUP):
                chunk_out(N_QUP + k, W_QUP + 2 * (k + 1), lambda t: qm[:, t, k * NC:(k + 1) * NC])
            for k in range(CH_KVUP):
                chunk_out(N_KVUP + k, W_KVUP + k + 1, lambda t: kvm[:, t, k * NC:(k + 1) * NC])

            def softmax_exp(n, i, step, scale):
                ring = n % 2
                act.wait_ge(prob_in, i * step + (n + 1))
                for t in range(NT):
                    lo, hi = (0, P) if t == 0 else (P, 3 * P)
                    ins = nc.scalar.activation(s_prob[:, ring, lo:hi], s_prob[:, ring, lo:hi], ACT.Exp,
                                               bias=nmax[:, ring, t:t + 1], scale=scale,
                                               accum_out=ssum[:, n % 4, t:t + 1])
                ins.then_inc(prob_ready, 1)

            def probs_out(n, i, step):
                act.wait_ge(o_in, i * step + (n + 1))
                act.wait_ge(pt_in, i * step + (n + 3))
                nc.scalar.copy(probT[:, n % 2, :], PS[:, 2 + n % 2, 0:384]).then_inc(pt_ready, 1)

            U = 2 * RPG
            with act.Fori(0, GROUPS) as g:
                act.wait_ge(heads_in, g * 2 + 1)
                nc.scalar.copy(qT.rearrange("p a t b -> p (a t b)"), PS[:, 6, :]).then_inc(qT_ready, 1)
                for n in range(U + 1):
                    if n < U:
                        softmax_exp(n, g, U, NSA_SCALE)
                    if n == 0:
                        act.wait_ge(cexp_in, g + 1)
                        nc.scalar.activation(csc[:, :, :], csc[:, :, :], ACT.Exp, scale=NSA_SCALE).then_inc(cexp_ready, 1)
                    if n >= 1:
                        probs_out(n - 1, g, U)
            with act.Fori(0, HEADS // MLA_BODY) as i:
                for n in range(MLA_BODY + 1):
                    if n < MLA_BODY:
                        softmax_exp(NSA_UNITS + n, i, MLA_BODY, MLA_SCALE)
                    if n >= 1:
                        probs_out(NSA_UNITS + n - 1, i, MLA_BODY)

            def bank_hi_out(n, dst):
                act.wait_ge(tr_done, n + 1)
                nc.scalar.copy(dst, PS[:, 4 + n % 4, :].rearrange("p (a b) -> p a b", b=P)).then_inc(bank_hi, 1)

            def w_high(m, i=None):
                k = 16 * ((m - W_BR) // SPLIT + 1)
                act.wait_ge(split_in[m % SPLIT], k if i is None else i * (16 * 8 // SPLIT) + k)
                nc.scalar.copy(w_hi[:, m % SPLIT, :, :], w_raw[:, m % SPLIT, :, :]).then_inc(hi_ready, 1)

            for n in range(NB_O, NB_O + TB_O, 2):
                a, t = oT_place(n - NB_O)
                bank_hi_out(n, oT_hi[:, a:a + 4, t * P:(t + 1) * P])
            for m in range(AHEAD):
                w_high(W_BR + m)
            with act.Fori(0, 4) as i:
                for m in range(AHEAD, AHEAD + 8):
                    w_high(W_BR + m, i)
            for n in range(NB_M, NB_M + TB_M, 2):
                a, t = h_place(n - NB_M)
                bank_hi_out(n, mergedT_hi[:, a:a + 4, t * P:(t + 1) * P])
            with act.Fori(0, 2) as i:
                for k in range(2):
                    for m in range(AHEAD, AHEAD + 8):
                        w_high(W_OUT + 8 * k + m, i * 2)
                    chunk_out(N_OUT + k, W_OUT + 8 * (k + 1), lambda t: y[:, t, bass.ds(i * (2 * NC) + k * NC, NC)],
                              ACT.Copy, i, 2, 8)
            root(3, RMS_Y, NT)
            for n in range(NB_SK, NB_SK + TB_SK, 2):
                bank_out(n, skT[:, 4 * (n - NB_SK):4 * (n - NB_SK) + 4, :])
            for t in range(NT):
                act.wait_ge(x1_ready, t + 1)
                nc.scalar.activation(at(o_t + 8 * t * KW, D), X[:, t, :], ACT.Square, scale=float(D) ** -0.5,
                                     accum_out=msq[:, RMS_X1 + t:RMS_X1 + t + 1]).then_inc(act_done, 1)
            act.wait_ge(act_done, NT)
            act.wait_ge(eps_ready, 1)
            nc.scalar.activation(rstd[:, RMS_X1:RMS_X1 + NT], msq[:, RMS_X1:RMS_X1 + NT], ACT.Sqrt,
                                 bias=eps[:, :]).then_inc(root_ready, 1)
            for n in range(NB_H2, NB_H2 + TB_H2, 2):
                a, t = h_place(n - NB_H2)
                bank_hi_out(n, h2T_hi[:, a:a + 4, t * P:(t + 1) * P])
            for n in range(4):
                for m in range(AHEAD, min(AHEAD + 8, 32 - 8 * n)):
                    w_high(W_PQ + 8 * n + m)
                act.wait_ge(w_used, W_PQ + 8 * (n + 1))
                for k in range(4):
                    ins = nc.scalar.copy(qryT[:, 4 * n + k, :], PS[:, 4 * (n % 2) + k, 0:SEQ])
                ins.then_inc(q_out, 1)
            def fetch(src):
                nc.scalar.copy(sst.rearrange("p s n -> p (s n)"), src).then_inc(sst_ready, 1)

            act.wait_ge(sc_in, 1)
            fetch(PS[:, 0, 0:2 * NK])
            for n in range(8):
                act.wait_ge(sc_in, n + 1)
                nc.scalar.copy(scores[:, n // 4, 2 * (n % 4):2 * (n % 4) + 2, :],
                               PS[:, n, :].rearrange("p (h n) -> p h n", h=2)).then_inc(sc_out, 1)

            act.wait_ge(sc_out, 8)
            scores_v = scores.rearrange("p t h n -> p (t h) n")

            def gate_exp(u):
                act.wait_ge(top_ready, u + 1)
                nc.scalar.activation(gate_e[:, :], top[:, 2, :], ACT.Exp, bias=gate_s[:, 0:1],
                                     accum_out=gate_s[:, 1:2]).then_inc(gexp_ready, 1)

            def unit(u, last=False):
                if not last:
                    act.wait_ge(idx_ready, u + 1)
                    fetch(scores_v[:, bass.ds(u + 1, 1), :].rearrange("p a n -> p (a n)"))
                for b in range(TOPK // BATCH):
                    cols = slice(b * BATCH, (b + 1) * BATCH)
                    act.wait_ge(u_free, u * TOPK + (RING + (b + 1) * BATCH))
                    nc.scalar.activation(act_g[:, cols], dots[:, cols], ACT.Gelu_apprx_tanh).then_inc(gelu_ready, 1)
                    if b == 2 and not last:
                        gate_exp(u + 1)
                    act.wait_ge(v_free, u * TOPK + (b + 1) * BATCH)
                    act.wait_ge(coef_ready, u * 4 + (b + 1))
                    for e in range(b * BATCH, (b + 1) * BATCH):
                        nc.scalar.activation(diag[e % 8], ident[:, :], ACT.Copy,
                                             scale=coef[:, e:e + 1]).then_inc(diag_ready, 1)

            def y_out(t):
                act.wait_ge(v_free, RING + (t + 1) * PH * TOPK)
                if t:
                    act.wait_ge(out_ready, t)
                nc.scalar.copy(yacc.rearrange("p (a b) -> p a b", a=4), PS[:, 4 * t:4 * t + 4, :]).then_inc(y_ready, 1)

            gate_exp(0)
            with act.Fori(0, PH) as u:
                unit(u)
            y_out(0)
            root(4, RMS_F, 1)
            with act.Fori(0, PH - 1) as u:
                unit(u + PH)
            unit(2 * PH - 1, True)
            y_out(1)
            root(5, RMS_F + 1, 1)

        @block.tensor
        def _(pe):
            def tile_ready(m, i=None, uses=0):
                v = 16 * (m // WSLOTS + 1)
                pe.wait_ge(w_landed[m % WSLOTS], v if i is None else i * (16 * uses) + v)

            def transposes(n, srcs):
                if n >= 4:
                    pe.wait_ge(tr_out[n % 2], n // 2 - 1)
                for k, s in enumerate(srcs):
                    r = s.shape[0]
                    ins = nc.tensor.transpose(PS[0:s.shape[1], 4 + n % 4, k * P:k * P + r], s, ident[0:r, 0:r])
                ins.then_inc(tr_done, 1)

            def column_sums(acc, m):
                for k in range(4):
                    ins = nc.tensor.matmul(PS[0:m, 4 + k, :], ones[:, 0:m], acc[:, k * NC:(k + 1) * NC],
                                           start=True, stop=True)
                ins.then_inc(ada_cols, 1)

            def split_tile_ready(m, i):
                pe.wait_ge(lo_ready, i * 16 + (m - W_BR + 1))

            def split_product(dst, a_hi, a_lo, b_hi, b_lo, start, stop):
                nc.tensor.matmul(dst, a_hi, b_hi, start=start, stop=False)
                nc.tensor.matmul(dst, a_hi, b_lo, start=False, stop=False)
                return nc.tensor.matmul(dst, a_lo, b_hi, start=False, stop=stop)

            def chunk(n, m, lhs, ktiles, cols=NC, i=None, step=0):
                if i is not None:
                    pe.wait_ge(pj_out, i * step + (n - 1))
                elif n >= 2:
                    pe.wait_ge(pj_out, n - 1)
                for w in range(ktiles // 2):
                    tile_ready(m + w, i, step)
                    for k in range(2):
                        for t in range(NT):
                            kk = 2 * w + k
                            ins = nc.tensor.matmul(PS[:, (n % 2) * 2 + t, 0:cols], lhs[:, kk, t * P:(t + 1) * P],
                                                   wring[:, (m + w) % WSLOTS, k, 0:cols],
                                                   start=(kk == 0), stop=(kk == ktiles - 1))
                    ins.then_inc(w_used, 1)

            pe.wait_ge(consts, 7)
            pe.wait_ge(pool_done, 5)
            for q in range(QTRS):
                if q:
                    banks_out(pe, 2 * q)
                for seg in range(2):
                    pe.wait_ge(ada_used, 8 * q + 4 * (seg + 1))
                    for odd in range(2):
                        ins = nc.tensor.matmul(PS[:, first_bank(q) + seg, :], ones[:, :], first_acc(seg, odd),
                                               start=(odd == 0), stop=(odd == 1))
                    ins.then_inc(ada_cols, 1)
                for t in range(NT):
                    pe.wait_ge(htok_ready, 2 * q + t + 1)
                    transposes(2 * q + t, [h_tok[:, t, (4 * q + k) * P:(4 * q + k + 1) * P] for k in range(4)])
                banks_out(pe, 2 * q + 2)
                for m in range(4 * q, 4 * q + 4):
                    tile_ready(m)
                    c_ = m // 2 % 2
                    for k in range(2):
                        for t in range(NT):
                            kk = 4 * q + 2 * (m % 2) + k
                            ins = nc.tensor.matmul(PS[:, 2 * c_ + t, :], hT[:, kk, t * P:(t + 1) * P],
                                                   wring[:, m % WSLOTS, k, :], start=(kk == 0), stop=(kk == KD - 1))
                    ins.then_inc(w_used, 1)

            with pe.Fori(0, (CH_MAIN - CH_FIRST) // 2) as i:
                for k in range(2):
                    chunk(2 + CH_FIRST + k, 8 * (CH_FIRST + k), hT, KD, i=i, step=2)
            chunk(2 + CH_MAIN, W_TAIL, hT, KD, cols=TAIL)
            with pe.Fori(0, 2) as i:
                for k in range(4):
                    chunk(2 + CH_MAIN + 1 + k, W_GATE + 8 * k, hT, KD, i=i, step=4)
                    if k % 2:
                        pe.wait_ge(ada_used, i * (2 * KD) + KD * (3 + k // 2))
                        pe.wait_ge(mod_ready, i * 2 + (k // 2 + 1))
                        column_sums(ada_acc[1 - k // 2], 1)

            pe.wait_ge(mod_ready, 5)
            transposes(NB_CMP, [cmp_rows[:, :]])
            pe.wait_ge(lat_ready, 1)
            for t in range(NT):
                transposes(NB_LAT + t, [proj[:, t, CQ0 + k * P:CQ0 + (k + 1) * P] for k in range(4)])
            transposes(NB_LAT + 2, [proj[:, t, CKV0 + k * P:CKV0 + (k + 1) * P] for k in range(2) for t in range(NT)])
            pe.wait_ge(pj_out, 2 + CH_MAIN + 1 + CH_GATE)
            pe.wait_ge(kdup_ready, 8)
            for b in range(4):
                for k in range(4):
                    g, t = 2 * (b % 2) + k // 2, k % 2
                    ins = nc.tensor.transpose(PS[:, b, k * P:(k + 1) * P],
                                              kdup[:, b // 2, t, g, :, :].rearrange("p a d -> p (a d)"), ident[:, :])
                ins.then_inc(kt2_in, 1)
            pe.wait_ge(kt2_ready, 4)
            for k in range(8):
                s = k // 4
                if k % 4 == 0:
                    pe.wait_ge(cmpx_ready, s + 1)
                tile_ready(W_CMP + k)
                for kk in range(4):
                    j = 4 * (k % 4) + kk
                    for h in range(2):
                        ins = nc.tensor.matmul(PS[:, 2 * s + h, 0:GROUPS * NCMP],
                                               w1ring[:, (W_CMP + k) % WSLOTS, kk, h * P:(h + 1) * P],
                                               cmpX[:, s, j, :], start=(j == 0), stop=(j == CB // 2 - 1))
                ins.then_inc(w_used, 1)
            pe.wait_ge(cmph_ready, 1)
            for h in range(2):
                ins = nc.tensor.matmul(PS[:, 0, 0:GROUPS * NCMP], w2k[:, h, :, :].rearrange("p a d -> p (a d)"),
                                       cmpH[:, 0, h, :], start=(h == 0), stop=(h == 1))
            ins.then_inc(cmpkv_in, 1)
            pe.wait_ge(cmprep_ready, 2)
            for g in range(GROUPS):
                for h in range(2):
                    ins = nc.tensor.matmul(PS[:, 2, g * HD:(g + 1) * HD],
                                           cmpHrep[:, h, g, :, :].rearrange("p a b -> p (a b)"), w2v[:, h, :],
                                           start=(h == 0), stop=(h == 1))
            ins.then_inc(cmpkv_in, 1)
            pe.wait_ge(cmpkv_ready, 2)
            banks_out(pe, NB_LAT + TB_LAT)
            for k in range(CH_QUP):
                chunk(2 + N_QUP + k, W_QUP + 2 * k, cqT, 4)
            for k in range(CH_KVUP):
                chunk(2 + N_KVUP + k, W_KVUP + k, ckvT, 2)

            def score(n, i, step, q, k):
                pe.wait_ge(s_free, i * step + (n + 1))
                nc.tensor.matmul(PS[:, n % 2, 0:P], q(0), k(0, P), start=True, stop=True)
                nc.tensor.matmul(PS[:, n % 2, P:3 * P], q(1), k(0, 2 * P), start=True, stop=True).then_inc(s_in, 1)

            def turn(n, i, step):
                pe.wait_ge(prob_ready, i * step + (n + 1))
                pe.wait_ge(pt_ready, i * step + (n + 1))
                for k in range(3):
                    ins = nc.tensor.transpose(PS[:, 2 + n % 2, k * P:(k + 1) * P], s_prob[:, n % 2, k * P:(k + 1) * P],
                                              ident[:, :])
                ins.then_inc(pt_in, 1)

            def weigh(n, i, step, v):
                pe.wait_ge(pt_ready, i * step + (n + 3))
                pe.wait_ge(o_free, i * step + (n + 1))
                nc.tensor.matmul(PS[:, 4 + n % 2, 0:HD], probT[:, n % 2, 0:P], v(0), start=True, stop=True)
                nc.tensor.matmul(PS[:, 4 + n % 2, HD:2 * HD], probT[:, n % 2, P:2 * P], v(0), start=True, stop=False)
                nc.tensor.matmul(PS[:, 4 + n % 2, HD:2 * HD], probT[:, n % 2, 2 * P:3 * P], v(1),
                                 start=False, stop=True).then_inc(o_in, 1)

            pe.wait_ge(pj_out, 2 + N_OUT)
            U = 2 * RPG
            with pe.Fori(0, GROUPS) as g:
                pe.wait_ge(staged, g * 6 + 6)
                for k in range(4):
                    ins = nc.tensor.transpose(PS[:, 6, k * P:(k + 1) * P], qst[:, k % 2, (k // 2) * P:(k // 2 + 1) * P],
                                              ident[:, :])
                ins.then_inc(heads_in, 1)
                for k in range(4):
                    ins = nc.tensor.transpose(PS[:, 7, k * P:(k + 1) * P],
                                              kst[:, k // 2, k % 2, :, :].rearrange("p a d -> p (a d)"), ident[:, :])
                ins.then_inc(heads_in, 1)
                pe.wait_ge(qT_ready, g + 1)
                pe.wait_ge(kT_ready, g + 1)
                for t in range(NT):
                    for r in range(RPG):
                        half = slice(HD * (r % 2), HD * (r % 2) + HD)
                        ins = nc.tensor.matmul(PS[:, 7 - r % 2, (t * RPG + r) * 16:(t * RPG + r) * 16 + NCMP],
                                               qT[half, r // 2, t, :], kcg[half, :], start=True, stop=True)
                        if t == NT - 1 and r >= RPG - 2:
                            ins.then_inc(csc_in, 1)
                for n in range(U + 2):
                    if n < U:
                        r, b = n // 2, n % 2
                        half = slice(HD * (r % 2), HD * (r % 2) + HD)
                        score(n, g, U, lambda t: qT[half, r // 2, t, :], lambda lo, hi: kT[half, b, lo:hi])
                    if 1 <= n <= U:
                        turn(n - 1, g, U)
                    if n == 2:
                        pe.wait_ge(cprob_ready, g + 1)
                        for t in range(NT):
                            ins = nc.tensor.transpose(PS[:, 6, t * P:(t + 1) * P],
                                                      Pc[:, t, :, :].rearrange("p r b -> p (r b)"), ident[:, :])
                        ins.then_inc(pct_in, 1)
                        pe.wait_ge(pct_ready, g + 1)
                        pe.wait_ge(cvalues_staged, g + 1)
                        for t in range(NT):
                            ins = nc.tensor.matmul(PS[:, 7, t * RPG * HD:(t + 1) * RPG * HD], PcT[:, t, :],
                                                   vcg.rearrange("p r d -> p (r d)"), start=True, stop=True)
                        ins.then_inc(oc_in, 1)
                    if n >= 2:
                        b = (n - 2) % 2
                        weigh(n - 2, g, U, lambda kt: proj[:, kt, bass.ds(
                            g * HD + (KV0 + ((b + 1) * 2 + 1) * GROUPS * HD), HD)])

            M = MLA_BODY
            with pe.Fori(0, HEADS // M) as i:
                def turn_heads(r):
                    pe.wait_ge(m_staged, i * (3 * M) + 3 * (r + 1))
                    pe.wait_ge(mt_ready, i * M + (r + 1))
                    for k in range(4):
                        ins = nc.tensor.transpose(PS[0:MD, 6 + r % 2, k * P:(k + 1) * P], mst[:, r % 2, k // 2, k % 2, :],
                                                  ident[:, :])
                    ins.then_inc(mt_in, 1)
                turn_heads(0)
                for n in range(M + 2):
                    if n + 1 < M:
                        turn_heads(n + 1)
                    if n < M:
                        pe.wait_ge(mt_ready, i * M + (n + 3))
                        score(NSA_UNITS + n, i, M, lambda t: mT[0:MD, n % 2, t, :],
                              lambda lo, hi: mT[0:MD, n % 2, 2:4, :].rearrange("p a b -> p (a b)")[:, lo:hi])
                    if 1 <= n <= M:
                        turn(NSA_UNITS + n - 1, i, M)
                    if n >= 2:
                        weigh(NSA_UNITS + n - 2, i, M, lambda kt: kvm[:, kt, bass.ds(
                            i * (M * 2 * MN) + (n - 2) * 2 * MN + MN, MN)])

            pe.wait_ge(grp_free, 1 + GROUPS + HEADS // M)
            pe.wait_ge(o_free, 2 + NSA_UNITS + HEADS)
            for n in range(TB_O):
                a, t = oT_place(n)
                src, j = (o_nsa, a) if a < 8 else (o_mla, a - 8)
                transposes(NB_O + n, [src[:, t, (j + k) * P:(j + k + 1) * P] for k in range(4)])
            banks_out(pe, NB_O + TB_O)

            with pe.Fori(0, 2) as i:
                for c_ in range(2):
                    pe.wait_ge(br_out, i * 2 + (c_ + 1))
                    for w in range(8):
                        m = W_BR + 8 * c_ + w
                        split_tile_ready(m, i)
                        for k in range(2):
                            for t in range(NT):
                                kk = 2 * (w % 4) + k
                                j, cols = 2 * w + k, slice(t * P, (t + 1) * P)
                                ins = split_product(PS[:, 4 * c_ + 2 * t + w // 4, :], oT_hi[:, j, cols], oT_lo[:, j, cols],
                                                    w_hi[:, m % SPLIT, k, :], w_lo[:, m % SPLIT, k, :],
                                                    start=(kk == 0), stop=(kk == 7))
                        ins.then_inc(w_used, 1)
            pe.wait_ge(br_out, 2 + 4)
            pe.wait_ge(merged_ready, 1)
            for n in range(TB_M):
                a, t = h_place(n)
                transposes(NB_M + n, [merged[:, t, (a + k) * P:(a + k + 1) * P] for k in range(4)])
            banks_out(pe, NB_M + TB_M)
            with pe.Fori(0, 2) as i:
                for c_ in range(2):
                    pe.wait_ge(pj_out, i * 2 + (2 + N_OUT + c_ - 1))
                    for w in range(8):
                        m = W_OUT + 8 * c_ + w
                        split_tile_ready(m, i)
                        for k in range(2):
                            for t in range(NT):
                                kk, cols = 2 * w + k, slice(t * P, (t + 1) * P)
                                ins = split_product(PS[:, ((N_OUT + c_) % 2) * 2 + t, :], mergedT_hi[:, kk, cols],
                                                    mergedT_lo[:, kk, cols], w_hi[:, m % SPLIT, k, :],
                                                    w_lo[:, m % SPLIT, k, :], start=(kk == 0), stop=(kk == KD - 1))
                        ins.then_inc(w_used, 1)

            pe.wait_ge(sk_in, 16 * 2 * PH)
            for n in range(TB_SK):
                transposes(NB_SK + n, [sk_raw[:, 4 * n + k, :] for k in range(4)])
            for n in range(TB_H2):
                a, t = h_place(n)
                pe.wait_ge(h2_ready, t + 1)
                transposes(NB_H2 + n, [h2[:, t, (a + k) * P:(a + k + 1) * P] for k in range(4)])
            banks_out(pe, NB_H2 + TB_H2)
            pe.wait_ge(pj_out, 2 + N_OUT + 4)
            with pe.Fori(0, 2) as i:
                for n in range(2):
                    pe.wait_ge(q_out, i * 2 + (n + 1))
                    for w in range(8):
                        m = W_PQ + 8 * n + w
                        split_tile_ready(m, i)
                        for k in range(2):
                            for blk in range(4):
                                kk, cols = 2 * w + k, slice(blk * P, (blk + 1) * P)
                                ins = split_product(PS[:, 4 * n + blk, 0:SEQ], w_hi[:, m % SPLIT, k, cols],
                                                    w_lo[:, m % SPLIT, k, cols], h2T_hi[:, kk, :], h2T_lo[:, kk, :],
                                                    start=(kk == 0), stop=(kk == KD - 1))
                        ins.then_inc(w_used, 1)
            pe.wait_ge(q_out, 2 + 4)
            for n in range(8):
                t = n // 4
                for k in range(4):
                    hp = 4 * (n % 4) + k
                    ins = nc.tensor.matmul(PS[:, n, k * NK:(k + 1) * NK], qryT[:, hp, t * P:(t + 1) * P], skT[:, hp, :],
                                           start=True, stop=True)
                ins.then_inc(sc_in, 1)
            pe.wait_ge(sc_out, 8)

            def unit(u, bank):
                for e in range(TOPK):
                    pe.wait_ge(v_in[e % RING], u * 32 + 16 * (e // RING + 1))
                    pe.wait_ge(diag_ready, u * TOPK + (e + 1))
                    for k in range(4):
                        ins = nc.tensor.matmul(PS[:, bank + k, :], diag[e % 8], Vrow[e % RING][:, k * NC:(k + 1) * NC],
                                               start=False, stop=False, skip_group_check=True)
                    ins.then_inc(v_free, 1)
            pe.wait_ge(zeros_ready, 1)
            for bank in range(8):
                nc.tensor.matmul(PS[:, bank, :], zeros, scores[:, 0, 0:2, :].rearrange("p h n -> p (h n)"),
                                 start=True, stop=True)
            for t in range(NT):
                with pe.Fori(0, PH) as u:
                    unit(u + t * PH, 4 * t)

        @block.vector
        def _(dve):
            v = nc.vector
            ch = Chain(dve, dve_done)
            link = ch.link

            for k, (s, n) in enumerate(((s_free, 2), (pt_in, 2), (o_in, 2), (o_free, 2), (pt_ready, 2), (mt_in, 2),
                                        (mt_ready, 2), (br_out, 2), (q_out, 2), (u_free, RING), (v_free, RING),
                                        (pj_out, 2), (mod_stored, 16), (mod_ready, 1))):
                v.memset(msq[:, k:k + 1], 0.0).then_inc(s, n)

            for k, s in enumerate((grp_free, idx_taken)):
                v.memset(rstd[:, k:k + 1], 0.0).then_inc(s, 1)

            def mean_square(col, src, junk):
                return v.tensor_tensor_reduce(junk, src, src, 1.0 / src.shape[-1], EPS, ALU.mult, ALU.add,
                                              msq[:, col:col + 1])

            def inverse_root(n, col, cnt):
                dve.wait_ge(root_ready, n)
                link(v.reciprocal(rstd[:, col:col + cnt], rstd[:, col:col + cnt]))

            v.memset(eps[:, :], EPS).then_inc(eps_ready, 1)

            dve.wait_ge(x_in, 16 * NT)
            dve.wait_ge(idx_taken, 1)
            for t in range(NT):
                ins = mean_square(RMS_X + t, X[:, t, :], h_tok[:, t, :])
            ins.then_inc(msq_ready, 1)
            inverse_root(1, RMS_X, NT)

            dve.wait_ge(silu_ready, 1)

            def segment(acc, uses, seg, i=None):
                for j in range(KD):
                    k = 16 * (uses + j // ADA_SLOTS + 1)
                    dve.wait_ge(ada_in[j % ADA_SLOTS], k if i is None else i * (16 * 2 * KD // ADA_SLOTS) + k)
                    w = ada_ring[:, j % ADA_SLOTS, :]
                    if j:
                        dve.wait_ge(ada_used, seg * KD + j if i is None else i * (2 * KD) + (seg * KD + j))
                        ins = v.scalar_tensor_tensor(out=acc, in0=w, scalar=csil[:, j:j + 1], in1=acc,
                                                     op0=ALU.mult, op1=ALU.add)
                    else:
                        ins = v.tensor_scalar(acc, w, csil[:, 0:1], None, ALU.mult)
                    ins.then_inc(ada_used, 1)

            def bank_out(n, dst):
                dve.wait_ge(tr_done, n + 1)
                v.tensor_copy(dst, PS[:, 4 + n % 4, :].rearrange("p (a b) -> p a b", b=P)).then_inc(tr_out[1], 1)
            for q in range(QTRS):
                cols = slice(q * NC, (q + 1) * NC)
                for n in range(8 * q, 8 * q + 8):
                    dve.wait_ge(ada_in[n % ADA_SLOTS], 16 * (n // ADA_SLOTS + 1))
                    for k in range(4):
                        j = 4 * (n % 4) + k
                        acc = first_acc(n // 4 % 2, k % 2)
                        w = ada_ring[:, n % ADA_SLOTS, k * NC:(k + 1) * NC]
                        if j >= 2:
                            if k == 1:
                                dve.wait_ge(ada_used, n)
                            else:
                                dve.wait_ge(dve_done, ch.n if k == 0 else ch.n - 1)
                            ins = v.scalar_tensor_tensor(out=acc, in0=w, scalar=csil[:, j:j + 1], in1=acc,
                                                         op0=ALU.mult, op1=ALU.add)
                        else:
                            ins = v.tensor_scalar(acc, w, csil[:, j:j + 1], None, ALU.mult)
                        ch.did(ins) if k < 3 else ins.then_inc(ada_used, 1)
                    if q and n == 8 * q:
                        bank_out(2 * q - 1, hT[:, 4 * q - 4:4 * q, P:2 * P])
                if q == 0:
                    dve.wait_ge(first_rows_in, 16 * 3)
                for seg, row in enumerate((shift_row, scale_row)):
                    dve.wait_ge(ada_cols, 2 * q + seg + 1)
                    ins = v.tensor_tensor(row[:, cols], row[:, cols], PS[:, first_bank(q) + seg, :], ALU.add)
                link(ins)
                link(v.scalar_tensor_tensor(out=scale_row[:, cols], in0=scale_row[:, cols], scalar=1.0,
                                            in1=gain_row[:, cols], op0=ALU.add, op1=ALU.mult))
                for t in range(NT):
                    link(v.scalar_tensor_tensor(out=h_tok[:, t, cols], in0=X[:, t, cols],
                                                scalar=rstd[:, RMS_X + t:RMS_X + t + 1], in1=scale_row[:, cols],
                                                op0=ALU.mult, op1=ALU.mult))
                    v.tensor_tensor(h_tok[:, t, cols], h_tok[:, t, cols], shift_row[:, cols], ALU.add).then_inc(htok_ready, 1)
            bank_out(TB_H - 1, hT[:, KD - 4:KD, P:2 * P])

            def reduced(r, k):
                link(v.tensor_scalar(ang[:, 2, :], ang[:, k, :], 1.0 / TWO_PI, None, ALU.mult))
                link(v.tensor_scalar(ang[:, 2, :], ang[:, 2, :], MAGIC, None, ALU.add))
                link(v.tensor_scalar(ang[:, 2, :], ang[:, 2, :], MAGIC, None, ALU.subtract))
                for part in PI_PARTS:
                    link(v.scalar_tensor_tensor(out=ang[:, r, :], in0=ang[:, 2, :], scalar=-part, in1=ang[:, r, :],
                                                op0=ALU.mult, op1=ALU.add))

            for k in range(16):
                f = float(np.float32(500000.0) ** np.float32(-k * (2.0 / MROPE)))
                ins = v.memset(freq[:, k:k + 1], f)
            link(ins)
            dve.wait_ge(small_in, 16 * 8)
            link(v.tensor_copy(pos_f[:, :], pos_i[:, :]))
            for t in range(NT):
                ins = v.tensor_scalar(ang[:, 0, t * 16:(t + 1) * 16], freq[:, :], pos_f[:, t:t + 1], None, ALU.mult)
            link(ins)
            reduced(0, 0)
            link(v.tensor_scalar(ang[:, 1, :], ang[:, 0, :], float(np.pi / 2), None, ALU.add))
            link(v.tensor_scalar(ang[:, 2, :], ang[:, 1, :], float(np.pi), -float(TWO_PI), ALU.is_gt, ALU.mult))
            link(v.tensor_tensor(ang[:, 1, :], ang[:, 1, :], ang[:, 2, :], ALU.add))
            v.tensor_scalar(ang[:, 0:2, :], ang[:, 0:2, :], PI_CLAMP, -PI_CLAMP, ALU.min, ALU.max).then_inc(angle_ready, 1)

            dve.wait_ge(htok_ready, QTRS * NT)
            with dve.Fori(0, 2) as i:
                for k in range(2):
                    dve.wait_ge(ada_cols, i * 2 + (2 * QTRS - 1 + k))
                    segment(ada_acc[1 - k], 4 * (2 + k), 2 + k, i)

            def rotate(parts, tmp, sin, cos):
                for a, b in [parts]:
                    v.tensor_tensor(tmp[0], a, cos, ALU.mult)
                    v.tensor_tensor(tmp[1], b, sin, ALU.mult)
                    v.tensor_tensor(tmp[2], b, cos, ALU.mult)
                    link(v.tensor_tensor(tmp[3], a, sin, ALU.mult))
                    v.tensor_tensor(a, tmp[0], tmp[1], ALU.subtract)
                    return v.tensor_tensor(b, tmp[2], tmp[3], ALU.add)

            dve.wait_ge(sin_ready, 2)
            dve.wait_ge(pj_out, 2 + CH_MAIN + CH_TAIL)
            H8 = NROPE // 2
            for t in range(NT):
                sin, cos = sincos[:, 0, t, 0:16:2], sincos[:, 1, t, 0:16:2]
                q = proj[:, t, Q0:KV0].rearrange("p (h d) -> p h d", d=HD)
                bc = lambda s_: s_.unsqueeze(1).to_broadcast([P, HEADS, H8])
                link(rotate((q[:, :, 0:H8], q[:, :, H8:NROPE]), [ropeT[:, k, t, :, :] for k in range(4)], bc(sin), bc(cos)))
                for b in range(3):
                    k0 = KV0 + b * 2 * GROUPS * HD
                    kk = proj[:, t, k0:k0 + GROUPS * HD].rearrange("p (g d) -> p g d", d=HD)
                    bk = lambda s_: s_.unsqueeze(1).to_broadcast([P, GROUPS, H8])
                    link(rotate((kk[:, :, 0:H8], kk[:, :, H8:NROPE]), [ropeT[:, k, t, 0:GROUPS, :] for k in range(4)],
                                bk(sin), bk(cos)))
            H16 = MROPE // 2
            kr = proj[:, :, KR0:KR0 + MROPE]
            tmp = [ropeT[:, k, :, 0:2, :].rearrange("p t a b -> p t (a b)") for k in range(4)]
            rotate((kr[:, :, 0:H16], kr[:, :, H16:MROPE]), tmp, sincos[:, 0, :, :], sincos[:, 1, :, :]).then_inc(rope_ready, 1)

            junk = at(o_a + 34 * KW, MQ)
            for n, (c0, w) in enumerate(((CQ0, MQ), (CKV0, MKV))):
                for t in range(NT):
                    link(mean_square(RMS_LAT + 2 * n + t, proj[:, t, c0:c0 + w], junk[:, 0:w]))
            dve.sem_inc(msq_ready, 1)
            inverse_root(2, RMS_LAT, 4)
            for n, (c0, w, g_row) in enumerate(((CQ0, MQ, qg_row), (CKV0, MKV, kvg_row))):
                for t in range(NT):
                    lat = proj[:, t, c0:c0 + w]
                    col = RMS_LAT + 2 * n + t
                    ins = v.scalar_tensor_tensor(out=lat, in0=lat, scalar=rstd[:, col:col + 1], in1=g_row[:, :],
                                                 op0=ALU.mult, op1=ALU.mult)
            ins.then_inc(lat_ready, 1)
            bank_out(NB_LAT, cqT[:, :, 0:P])
            dve.wait_ge(tr_done, NB_LAT + 3)
            v.tensor_copy(ckvT.rearrange("p j t -> p (j t)"), PS[:, 4 + (NB_LAT + 2) % 4, :]).then_inc(tr_out[1], 1)

            for b in range(4):
                dve.wait_ge(kt2_in, b + 1)
                ins = v.tensor_copy(KT2[0:HD, b // 2, 2 * (b % 2):2 * (b % 2) + 2, :],
                                    PS[0:HD, b, :].rearrange("p (g t) -> p g t", g=2))
            link(ins)
            dve.wait_ge(kt2_ready, 4)
            dve.wait_ge(tr_out[0], NB_CMP // 2 + 1)
            for s in range(2):
                for hi in range(2):
                    raw = KT2[:, s, :, :].rearrange("p g (b l) -> p l g b", l=CS)[:, 0:CS:2, :, hi:hi + NCMP]
                    pe_c = cmp_cols[:, s * 16 + hi * 8:s * 16 + hi * 8 + 8]
                    pe_c = pe_c.unsqueeze(2).unsqueeze(3).to_broadcast([P, 8, GROUPS, NCMP])
                    ins = v.tensor_tensor(cmpX[:, s, hi * 8:hi * 8 + 8, :].rearrange("p l (g b) -> p l g b", g=GROUPS),
                                          raw, pe_c, ALU.add)
                ins.then_inc(cmpx_ready, 1)
            link(v.memset(cmpHrep, 0.0))
            link(v.memset(Pc, 0.0))
            dve.wait_ge(cmph_ready, 2)
            for h in range(2):
                src = cmpH[:, 1, h, :].rearrange("p (g b) -> p g b", g=GROUPS)
                for copy in range(4):
                    ins = v.tensor_copy(cmpHrep[:, h, :, copy, 0:NCMP], src)
                ins.then_inc(cmprep_ready, 1)
            dve.wait_ge(cmpkv_in, 1)
            v.tensor_copy(kcT.rearrange("p g b -> p (g b)"), PS[:, 0, 0:GROUPS * NCMP]).then_inc(cmpkv_ready, 1)
            dve.wait_ge(cmpkv_in, 2)
            v.tensor_copy(vc.rearrange("p g d -> p (g d)"), PS[:, 2, 0:GROUPS * HD]).then_inc(cmpkv_ready, 1)
            dve.wait_ge(pj_out, 2 + N_KVUP)
            for t in range(NT):
                q = qm[:, t, :].rearrange("p (h d) -> p h d", d=MD)
                bc = lambda s_: s_.unsqueeze(1).to_broadcast([P, HEADS, H16])
                tmp = [at(o_r + (8 + k) * KW, HEADS, H16) for k in range(4)]
                ins = rotate((q[:, :, MN:MN + H16], q[:, :, MN + H16:MD]), tmp, bc(sincos[:, 0, t, :]), bc(sincos[:, 1, t, :]))
                link(ins) if t == 0 else ins.then_inc(qm_roped, 1)

            def mask_max(n, i, step):
                r = n % 2
                dve.wait_ge(s_in, i * step + (n + 1))
                dve.wait_ge(pt_in, i * step + (n + 1))
                dve.sem_inc(dve_passed, 1)
                v.tensor_tensor_reduce(s_prob[:, r, 0:P], PS[:, r, 0:P], causal[:, P:2 * P], 1.0, NEG * 3, ALU.add,
                                       ALU.max, smax[:, r, 0:1])
                v.tensor_tensor_reduce(s_prob[:, r, P:3 * P], PS[:, r, P:3 * P], causal[:, :], 1.0, NEG * 3, ALU.add,
                                       ALU.max, smax[:, r, 1:2]).then_inc(s_free, 1)
                dve.wait_ge(s_free, i * step + (n + 3))

            def minus_max(n, scale):
                v.tensor_scalar(nmax[:, n % 2, :], smax[:, n % 2, :], -scale, None, ALU.mult).then_inc(prob_in, 1)

            def output(n, i, step, place, gate=None):
                dve.wait_ge(prob_ready, i * step + (n + 1))
                link(v.reciprocal(srec[:, n % 2, :], ssum[:, n % 4, :]))
                if gate is not None:
                    link(v.tensor_tensor(srec[:, n % 2, :], srec[:, n % 2, :], gate, ALU.mult))
                dve.wait_ge(o_in, i * step + (n + 3))
                for t in range(NT):
                    src = PS[:, 4 + n % 2, t * HD:(t + 1) * HD]
                    if gate is None:
                        ins = v.tensor_scalar(place(t), src, srec[:, n % 2, t:t + 1], None, ALU.mult)
                    else:
                        ins = v.scalar_tensor_tensor(out=place(t), in0=src, scalar=srec[:, n % 2, t:t + 1], in1=place(t),
                                                     op0=ALU.mult, op1=ALU.add)
                ins.then_inc(o_free, 1)

            U = 2 * RPG
            with dve.Fori(0, GROUPS) as g:
                ch.enter(g, 22)
                dve.wait_ge(heads_in, g * 2 + 2)
                v.tensor_copy(kT.rearrange("p b t -> p (b t)"), PS[:, 7, :]).then_inc(kT_ready, 1)
                csc4 = csc[:, :, :].rearrange("p (t r) b -> p t r b", t=NT)

                def compressed_max():
                    dve.wait_ge(csc_in, g * 2 + 2)
                    cm = cmask[:, :, :].unsqueeze(2).to_broadcast([P, NT, RPG // 2, NCMP])
                    for odd in range(2):
                        cps = PS[:, 7 - odd, 0:P].rearrange("p (t r b) -> p t r b", t=NT, r=RPG)[:, :, odd:RPG:2, 0:NCMP]
                        ins = v.tensor_tensor(csc4[:, :, odd:RPG:2, :], cps, cm, ALU.add)
                    link(ins)
                    link(v.tensor_reduce(cstat[:, 0, :], csc[:, :, :], AX_X, ALU.max))
                    v.tensor_tensor(csc[:, :, :], csc[:, :, :], cstat[:, 0, :].unsqueeze(2).to_broadcast([P, 8, NCMP]),
                                    ALU.subtract).then_inc(cexp_in, 1)

                def compressed_probs():
                    dve.wait_ge(gates_staged, g + 1)
                    cm01 = cmask01[:, :, :].unsqueeze(2).to_broadcast([P, NT, RPG, NCMP])
                    dve.wait_ge(cexp_ready, g + 1)
                    link(v.tensor_reduce(cstat[:, 1, :], csc[:, :, :], AX_X, ALU.add))
                    link(v.reciprocal(cstat[:, 2, :], cstat[:, 1, :]))
                    gate0 = gst[:, :, 0:3 * RPG:3]
                    link(v.tensor_tensor(cstat[:, 3, :].rearrange("p (t r) -> p t r", t=NT),
                                         cstat[:, 2, :].rearrange("p (t r) -> p t r", t=NT), gate0, ALU.mult))
                    link(v.tensor_tensor(csc[:, :, :], csc[:, :, :], cstat[:, 3, :].unsqueeze(2).to_broadcast([P, 8, NCMP]),
                                         ALU.mult))
                    v.tensor_tensor(Pc[:, :, :, 0:NCMP], csc4, cm01, ALU.mult).then_inc(cprob_ready, 1)

                for n in range(U + 2):
                    if n < U:
                        mask_max(n, g, U)
                        minus_max(n, NSA_SCALE)
                    if n == 0:
                        compressed_max()
                    if n == 1:
                        compressed_probs()
                        dve.wait_ge(grp_free, g + 1)
                    if n == 2:
                        dve.wait_ge(pct_in, g + 1)
                        v.tensor_copy(PcT.rearrange("p t q -> p (t q)"), PS[:, 6, 0:2 * P]).then_inc(pct_ready, 1)
                        dve.wait_ge(oc_in, g + 1)
                        for t in range(NT):
                            ins = v.tensor_copy(ogrp[:, t, 0:RPG, :],
                                                PS[:, 7, t * RPG * HD:(t + 1) * RPG * HD].rearrange("p (r d) -> p r d", d=HD))
                    if n >= 2:
                        r, b = (n - 2) // 2, (n - 2) % 2
                        output(n - 2, g, U, lambda t: ogrp[:, t, r, :], gst[:, :, 3 * r + b + 1])
                dve.wait_ge(o_free, g * U + (U + 2))
                v.memset(smax[:, 0, :], 0.0).then_inc(grp_ready, 1)
                ch.leave(GROUPS)

            M = MLA_BODY
            with dve.Fori(0, HEADS // M) as i:
                ch.enter(i, 8)
                def heads_out(r):
                    dve.wait_ge(mt_in, i * M + (r + 3))
                    v.tensor_copy(mT[0:MD, r % 2, :, :].rearrange("p a b -> p (a b)"), PS[0:MD, 6 + r % 2, :]).then_inc(
                        mt_ready, 1)
                dve.wait_ge(grp_free, i + (GROUPS + 1))
                heads_out(0)
                for n in range(M + 2):
                    if n + 1 < M:
                        if n >= 1:
                            dve.wait_ge(s_in, i * M + (NSA_UNITS + n))
                        heads_out(n + 1)
                    if n < M:
                        mask_max(NSA_UNITS + n, i, M)
                        minus_max(NSA_UNITS + n, MLA_SCALE)
                    if n >= 2:
                        output(NSA_UNITS + n - 2, i, M, lambda t: ogrp[:, t, n - 2, :])
                dve.wait_ge(o_free, i * M + (NSA_UNITS + M + 2))
                v.memset(smax[:, 0, :], 0.0).then_inc(grp_ready, 1)
                ch.leave(HEADS // M)

            def banks_split(first, taken, place, hi, lo):
                for n in range(first, first + 8):
                    a, t = place(n - first)
                    src = PS[:, 4 + n % 4, :].rearrange("p (a b) -> p a b", b=P)
                    high, low = hi[:, a:a + 4, t * P:(t + 1) * P], lo[:, a:a + 4, t * P:(t + 1) * P]
                    if n % 2 == first % 2:
                        dve.wait_ge(bank_hi, taken + (n - first) // 2 + 1)
                    else:
                        dve.wait_ge(tr_done, n + 1)
                        link(v.tensor_copy(high, src))
                    v.tensor_tensor(low, src, high.bitcast(F32), ALU.subtract).then_inc(tr_out[n % 2], 1)

            def w_low(m, i=None):
                dve.wait_ge(hi_ready, m - W_BR + 1 if i is None else i * 8 + (m - W_BR + 1))
                v.tensor_tensor(w_lo[:, m % SPLIT, :, :], w_raw[:, m % SPLIT, :, :],
                                w_hi[:, m % SPLIT, :, :].bitcast(F32), ALU.subtract).then_inc(lo_ready, 1)

            banks_split(NB_O, 0, oT_place, oT_hi, oT_lo)
            for m in range(AHEAD):
                w_low(W_BR + m)

            with dve.Fori(0, 2) as i:
                ch.enter(i, 8)
                for c_ in range(2):
                    for m in range(AHEAD, AHEAD + 8):
                        w_low(W_BR + 8 * c_ + m, i * 2)
                    dve.wait_ge(w_used, i * 16 + (W_BR + 8 * (c_ + 1)))
                    for t in range(NT):
                        cols = bass.ds(i * (2 * NC) + c_ * NC, NC)
                        for b in range(2):
                            ins = v.tensor_tensor(mtmp[:, t, b, :], PS[:, 4 * c_ + 2 * t + b, :], gates[:, t, b, cols],
                                                  ALU.mult)
                            if t == NT - 1 and b == 1:
                                ins.then_inc(br_out, 1)
                            else:
                                ch.did(ins)
                    dve.wait_ge(br_out, i * 2 + (c_ + 3))
                    ch.wait()
                    for t in range(NT):
                        ins = v.tensor_tensor(merged[:, t, cols], mtmp[:, t, 0, :], mtmp[:, t, 1, :], ALU.add)
                    link(ins)
                ch.leave(2)
            ch.wait()
            v.memset(smax[:, 0, :], 0.0).then_inc(merged_ready, 1)
            banks_split(NB_M, TB_O // 2, h_place, mergedT_hi, mergedT_lo)

            dve.wait_ge(rows_ready, 1)
            for n in range(D // NC):
                for m in range(AHEAD, AHEAD + 8):
                    w_low(W_OUT + 8 * n + m)
                dve.wait_ge(pj_out, 2 + N_OUT + n + 1)
                for t in range(NT):
                    part = y[:, t, n * NC:(n + 1) * NC]
                    ch.did(v.tensor_tensor_reduce(at(o_g + t * NC, NC), part, part, 1.0 / D, 0.0, ALU.mult, ALU.add,
                                                  ysq[:, t, n:n + 1]))
                ch.wait()
                for t in range(NT):
                    part = y[:, t, n * NC:(n + 1) * NC]
                    ch.did(v.tensor_tensor(part, part, gate_a_row[:, n * NC:(n + 1) * NC], ALU.mult))
            link(v.tensor_reduce(msq[:, RMS_Y:RMS_Y + NT], ysq[:, :, :], AX_X, ALU.add))
            v.tensor_scalar(msq[:, RMS_Y:RMS_Y + NT], msq[:, RMS_Y:RMS_Y + NT], EPS, None, ALU.add).then_inc(msq_ready, 1)
            for n in range(NB_SK + 1, NB_SK + TB_SK, 2):
                bank_out(n, skT[:, 4 * (n - NB_SK):4 * (n - NB_SK) + 4, :])
            inverse_root(3, RMS_Y, NT)

            def add_branch(t, src, col, row):
                link(v.scalar_tensor_tensor(out=src, in0=src, scalar=rstd[:, col:col + 1], in1=row,
                                            op0=ALU.mult, op1=ALU.mult))
                return v.tensor_tensor(X[:, t, :], X[:, t, :], src, ALU.add)
            for t in range(NT):
                v.scalar_tensor_tensor(out=X[:, t, :], in0=y[:, t, :], scalar=rstd[:, RMS_Y + t:RMS_Y + t + 1],
                                       in1=X[:, t, :], op0=ALU.mult, op1=ALU.add).then_inc(x1_ready, 1)
            dve.wait_ge(x1_ready, NT)
            dve.wait_ge(rows_ready, 2)
            for t in range(NT):
                link(v.tensor_tensor(h2[:, t, :], X[:, t, :], scale_f_row, ALU.mult))
            inverse_root(4, RMS_X1, NT)
            for t in range(NT):
                v.scalar_tensor_tensor(out=h2[:, t, :], in0=h2[:, t, :], scalar=rstd[:, RMS_X1 + t:RMS_X1 + t + 1],
                                       in1=shift_f_row, op0=ALU.mult, op1=ALU.add).then_inc(h2_ready, 1)
            banks_split(NB_H2, (TB_O + TB_M) // 2, h_place, h2T_hi, h2T_lo)
            for m in range(AHEAD, 32):
                w_low(W_PQ + m)
            dve.wait_ge(last_row_in, 48)
            link(v.tensor_tensor(gate_f_row, gate_f_row, bias_tmp, ALU.add))
            link(v.tensor_tensor(gate_f_row, gate_f_row, yacc, ALU.mult))
            v.memset(zeros, 0.0).then_inc(zeros_ready, 1)

            dve.wait_ge(consts, 7)
            link(v.tensor_copy(iota_f[:, :], iota_i[:, :]))

            def settled():
                ch.wait()
                dve.sem_inc(dve_passed, 1)

            def top16(row, values, work):
                ch.did(v.max(top[:, row, 0:8], values))
                settled()
                v.max_index(topi[:, row, 0:8], top[:, row, 0:8], values)
                ch.did(v.match_replace(work, top[:, row, 0:8], values, -3e38))
                settled()
                ch.did(v.max(top[:, row, 8:16], work))
                settled()
                ch.did(v.max_index(topi[:, row, 8:16], top[:, row, 8:16], work))
                settled()

            def topk_parts(u):
                def halves(s):
                    if s == 0:
                        dve.wait_ge(idx_taken, u + 1)
                        dve.wait_ge(sst_ready, u + 1)
                        dve.sem_inc(dve_passed, 1)
                    top16(s, sst[:, s, :], stmp[:, 0:NK])

                def candidates():
                    link(v.tensor_tensor(cand, top[:, 0, :].unsqueeze(2).to_broadcast([P, TOPK, TOPK]),
                                         top[:, 1, :].unsqueeze(1).to_broadcast([P, TOPK, TOPK]), ALU.add))
                    dve.sem_inc(dve_passed, 1)
                    top16(2, cand.rearrange("p a b -> p (a b)"), stmp)
                    v.tensor_scalar(gate_s[:, 0:1], top[:, 2, 0:1], -1.0, None, ALU.mult).then_inc(top_ready, 1)

                def experts():
                    ch.did(v.tensor_scalar(ab_u[:, 0, :], topi[:, 2, :], 4, None, ALU.logical_shift_right))
                    ch.did(v.tensor_scalar(ab_u[:, 1, :], topi[:, 2, :], TOPK - 1, None, ALU.bitwise_and))
                    link(v.tensor_copy(topf[:, :, :], topi[:, 0:2, :]))
                    link(v.tensor_copy(ab_f[:, :, :], ab_u[:, :, :]))
                    link(v.tensor_tensor(onehot, ab_f[:, :, :].unsqueeze(3).to_broadcast([P, 2, TOPK, TOPK]),
                                         iota_f[:, :].unsqueeze(1).unsqueeze(1).to_broadcast([P, 2, TOPK, TOPK]),
                                         ALU.is_equal))
                    link(v.tensor_tensor(onehot, onehot, topf[:, :, :].unsqueeze(2).to_broadcast([P, 2, TOPK, TOPK]),
                                         ALU.mult))
                    link(v.tensor_reduce(i12[:, :, :], onehot, AX_X, ALU.add))
                    v.scalar_tensor_tensor(out=idx_next[:, :], in0=i12[:, 0, :], scalar=float(NK), in1=i12[:, 1, :],
                                           op0=ALU.mult, op1=ALU.add).then_inc(idx_ready, 1)
                    dve.wait_ge(gexp_ready, u + 1)
                    link(v.reciprocal(gate_s[:, 2:3], gate_s[:, 1:2]))
                    link(v.tensor_scalar(gate_next[:, :], gate_e[:, :], gate_s[:, 2:3], None, ALU.mult))

                return [lambda: halves(0), lambda: halves(1), candidates, experts]

            TOPK_STEPS = 22

            def unit(u, t, last=False):
                link(v.tensor_copy(gate_now[:, :], gate_next[:, :]))
                parts = [] if last else topk_parts(u + 1)

                def coefs(b):
                    cols = slice(b * BATCH, (b + 1) * BATCH)
                    dve.wait_ge(gelu_ready, u * 4 + (b + 1))
                    v.tensor_tensor(coef[:, cols], act_g[:, cols], gate_now[:, cols], ALU.mult).then_inc(coef_ready, 1)
                for b in range(TOPK // BATCH):
                    for e in range(b * BATCH, (b + 1) * BATCH):
                        dve.wait_ge(u_in[e % RING], u * 32 + 16 * (e // RING + 1))
                        row = Urow[e % RING]
                        v.tensor_tensor_reduce(row, row, h2[:, t, :], 1.0, 0.0, ALU.mult, ALU.add,
                                               dots[:, e:e + 1]).then_inc(u_free, 1)
                    if parts:
                        parts[b]()
                    coefs(b)
                dve.wait_ge(coef_ready, u * 4 + 4)

            def finish(t):
                dve.wait_ge(y_ready, t + 1)
                v.tensor_tensor_reduce(PS[:, 4 * t:4 * t + 4, :].rearrange("p a b -> p (a b)"), yacc, yacc, 1.0 / D, EPS,
                                       ALU.mult, ALU.add, msq[:, RMS_F + t:RMS_F + t + 1]).then_inc(msq_ready, 1)
                inverse_root(5 + t, RMS_F + t, 1)
                add_branch(t, yacc, RMS_F + t, gate_f_row).then_inc(out_ready, 1)

            for part in topk_parts(0):
                part()
            with dve.Fori(0, PH) as u:
                ch.enter(u, TOPK_STEPS + 1)
                unit(u, 0)
                ch.leave(PH)
            finish(0)
            with dve.Fori(0, PH - 1) as u:
                ch.enter(u, TOPK_STEPS + 1)
                unit(u + PH, 1)
                ch.leave(PH - 1)
            unit(2 * PH - 1, 1, last=True)
            finish(1)


_INS = ["x", "c", "positions", "ada_w", "ada_b", "attn_pre_g", "attn_post_g", "w_in", "cmp_pe", "cmp_w1", "cmp_b1",
        "cmp_w2", "mla_q_norm_g", "mla_w_q_up", "mla_kv_norm_g", "mla_w_kv_up", "w_branch_nsa", "w_branch_mla", "w_out",
        "ffn_pre_g", "ffn_post_g", "peer_w_q", "peer_sub_keys", "peer_u", "peer_v"]


def kernel(**inputs):
    import numpy as _np
    import concourse.bacc as _bacc
    from concourse import mybir as _mybir
    from concourse.bass_utils import run_bass_kernel_spmd as _run

    nc = _bacc.Bacc("TRN2", target_bir_lowering=False, num_devices=1)
    arrays, args = {}, []
    for name in _INS:
        a = _np.ascontiguousarray(inputs[name])
        arrays[f"in_{name}_dram"] = a
        args.append(nc.dram_tensor(f"in_{name}_dram", a.shape, _mybir.dt.from_np(a.dtype), kind="ExternalInput").ap())
    out = nc.dram_tensor("out_0_dram", (1, SEQ, D), _mybir.dt.float32, kind="ExternalOutput").ap()
    build(nc, *args, out)
    r = _run(nc, [arrays], core_ids=[0])
    return r.results[0]["out_0_dram"]
```
